# Optimizing a Trainium2 kernel written in Bass

```python
import math
import jax, jax.numpy as jnp
from jax import lax
import numpy as np

D_MODEL = 1024
BATCH = 1
SEQ = 512
DEPTH = 2

GRID_W = 64
CTX_LEN = 256
HEAD_DIM = 64
ROPE_THETA = 10000.0
EPS = 1e-6
Q_BLOCK = 128
A_Q_HEADS = 8
A_KV_HEADS = 2
A_WIDTH = A_Q_HEADS * HEAD_DIM
A_KV_WIDTH = A_KV_HEADS * HEAD_DIM
B_WIDTH = D_MODEL // 2
B_WINDOWS = (2, 4, 8, 16)
B_GROUPS = len(B_WINDOWS)
B_GROUP_W = B_WIDTH // B_GROUPS
EVEN_IN = A_WIDTH + 2 * A_KV_WIDTH + B_WIDTH
EVEN_MIX = A_WIDTH + B_WIDTH
C_Q_HEADS = 16
C_KV_HEADS = 4
C_WIDTH = C_Q_HEADS * HEAD_DIM
C_KV_WIDTH = C_KV_HEADS * HEAD_DIM
ODD_IN = C_WIDTH + 2 * C_KV_WIDTH
WINDOW = 128
N_SIDE = WINDOW // Q_BLOCK
BAND_BLOCKS = 2 * N_SIDE + 1
BAND_LEN = BAND_BLOCKS * Q_BLOCK
FFN_HIDDEN = int(math.ceil(8 * D_MODEL / 3 / 256)) * 256
N_EVEN = (DEPTH + 1) // 2
N_ODD = DEPTH // 2


def rmsnorm(x, g):
    xf = x.astype(jnp.float32)
    y = xf * lax.rsqrt(jnp.mean(xf * xf, axis=-1, keepdims=True) + EPS)
    return (y * g.astype(jnp.float32)).astype(x.dtype)

def modulate(x, g, shift, scale):
    return rmsnorm(x, g) * (1 + scale) + shift

def split_heads(t, h):
    return t.reshape(t.shape[0], t.shape[1], h, HEAD_DIM)

def axial_rope(x, rows, cols):
    hd = x.shape[-1]
    quarter = hd // 4
    freqs = ROPE_THETA ** (-jnp.arange(quarter, dtype=jnp.float32) / quarter)

    def rot(a, pos):
        ang = pos.astype(jnp.float32)[:, None] * freqs[None, :]
        cos = jnp.cos(ang)[None, :, None, :]
        sin = jnp.sin(ang)[None, :, None, :]
        a1, a2 = a[..., :quarter], a[..., quarter:]
        return jnp.concatenate([a1 * cos - a2 * sin, a2 * cos + a1 * sin], axis=-1)

    out = jnp.concatenate([rot(x[..., :hd // 2], rows), rot(x[..., hd // 2:], cols)], axis=-1)
    return out.astype(x.dtype)

def dense_gqa_blocks(q, k, v):
    B, S, H, hd = q.shape
    KV = k.shape[2]
    G = H // KV
    nb = S // Q_BLOCK
    scale = 1.0 / math.sqrt(hd)
    qb = q.reshape(B, nb, Q_BLOCK, KV, G, hd).transpose(1, 0, 2, 3, 4, 5)

    def one(qblk):
        s = jnp.einsum('bqkgd,btkd->bkgqt', qblk, k, preferred_element_type=jnp.float32) * scale
        p = jax.nn.softmax(s, axis=-1).astype(v.dtype)
        return jnp.einsum('bkgqt,btkd->bqkgd', p, v)

    o = lax.map(one, qb)
    return o.transpose(1, 0, 2, 3, 4, 5).reshape(B, S, H * hd)

def ctx_attention(q, k, v, sink=None):
    B, T, H, hd = q.shape
    KV = k.shape[2]
    G = H // KV
    scale = 1.0 / math.sqrt(hd)
    qg = q.reshape(B, T, KV, G, hd)
    s = jnp.einsum('bqkgd,btkd->bkgqt', qg, k, preferred_element_type=jnp.float32) * scale
    if sink is not None:
        s_sink = jnp.broadcast_to(sink.reshape(KV, G)[None, :, :, None, None].astype(jnp.float32),
                                  (B, KV, G, T, 1))
        s = jnp.concatenate([s, s_sink], axis=-1)
    p = jax.nn.softmax(s, axis=-1)
    if sink is not None:
        p = p[..., :-1]
    o = jnp.einsum('bkgqt,btkd->bqkgd', p.astype(v.dtype), v)
    return o.reshape(B, T, H * hd)

def window_gqa_blocks(q, k, v, k_ctx, v_ctx, sink):
    B, S, H, hd = q.shape
    KV = k.shape[2]
    G = H // KV
    C = k_ctx.shape[1]
    nb = S // Q_BLOCK
    scale = 1.0 / math.sqrt(hd)
    qb = q.reshape(B, nb, Q_BLOCK, KV, G, hd).transpose(1, 0, 2, 3, 4, 5)

    def band(t):
        tp = jnp.pad(t, ((0, 0), (WINDOW, WINDOW), (0, 0), (0, 0)))
        tp = tp.reshape(B, nb + 2 * N_SIDE, Q_BLOCK, KV, hd)
        tb = jnp.concatenate([tp[:, j:j + nb] for j in range(BAND_BLOCKS)], axis=2)
        return tb.transpose(1, 0, 2, 3, 4)

    kb, vb = band(k), band(v)
    n_i = jnp.arange(nb)[:, None, None]
    q_i = jnp.arange(Q_BLOCK)[None, :, None]
    k_j = jnp.arange(BAND_LEN)[None, None, :]
    qpos = n_i * Q_BLOCK + q_i
    kpos = n_i * Q_BLOCK - WINDOW + k_j
    mask = (kpos >= 0) & (kpos < S) & (jnp.abs(qpos - kpos) <= WINDOW)
    sink_l = sink.reshape(KV, G)[None, :, :, None, None].astype(jnp.float32)

    def one(args):
        qblk, kblk, vblk, m = args
        s_w = jnp.einsum('bqkgd,btkd->bkgqt', qblk, kblk, preferred_element_type=jnp.float32) * scale
        s_w = jnp.where(m[None, None, None], s_w, -jnp.inf)
        s_c = jnp.einsum('bqkgd,btkd->bkgqt', qblk, k_ctx, preferred_element_type=jnp.float32) * scale
        s_s = jnp.broadcast_to(sink_l, (B, KV, G, Q_BLOCK, 1))
        p = jax.nn.softmax(jnp.concatenate([s_w, s_c, s_s], axis=-1), axis=-1).astype(v.dtype)
        o = jnp.einsum('bkgqt,btkd->bqkgd', p[..., :BAND_LEN], vblk)
        o = o + jnp.einsum('bkgqt,btkd->bqkgd', p[..., BAND_LEN:BAND_LEN + C], v_ctx)
        return o

    o = lax.map(one, (qb, kb, vb, mask))
    return o.transpose(1, 0, 2, 3, 4, 5).reshape(B, S, H * hd)

def centred_mean(u, w):
    S = u.shape[1]
    cs = jnp.pad(jnp.cumsum(u.astype(jnp.float32), axis=1), ((0, 0), (1, 0), (0, 0)))
    t = jnp.arange(S)
    lo = jnp.clip(t - w // 2, 0, S)
    hi = jnp.clip(t + w - w // 2, 0, S)
    cnt = (hi - lo).astype(jnp.float32)
    return ((cs[:, hi] - cs[:, lo]) / cnt[None, :, None]).astype(u.dtype)

def pool_mixer(u, w_pool, pool_scale):
    B, S, _ = u.shape
    diffs = []
    for g, w in enumerate(B_WINDOWS):
        ug = u[..., g * B_GROUP_W:(g + 1) * B_GROUP_W]
        diffs.append(centred_mean(ug, w) - ug)
    d = jnp.stack(diffs, axis=2)
    y = jnp.einsum('bsgc,gcd->bsgd', d, w_pool).reshape(B, S, B_WIDTH)
    return y * pool_scale

def even_mixer(h, hc, w_in, w_out, q_gain, k_gain, w_pool, pool_scale, rows, cols, with_ctx):
    def project(t):
        p = t @ w_in
        q, k, v, u = jnp.split(p, [A_WIDTH, A_WIDTH + A_KV_WIDTH, A_WIDTH + 2 * A_KV_WIDTH], axis=-1)
        q = rmsnorm(split_heads(q, A_Q_HEADS), q_gain)
        k = rmsnorm(split_heads(k, A_KV_HEADS), k_gain)
        return q, k, split_heads(v, A_KV_HEADS), u

    q, k, v, u = project(h)
    qc, kc, vc, uc = project(hc)
    q = axial_rope(q, rows, cols)
    k = axial_rope(k, rows, cols)
    a = dense_gqa_blocks(q, jnp.concatenate([k, kc], axis=1), jnp.concatenate([v, vc], axis=1))
    b = pool_mixer(u, w_pool, pool_scale)
    y = jnp.concatenate([a, b], axis=-1) @ w_out
    yc = None
    if with_ctx:
        ac = ctx_attention(qc, kc, vc)
        bc = pool_mixer(uc, w_pool, pool_scale)
        yc = jnp.concatenate([ac, bc], axis=-1) @ w_out
    return y, yc

def odd_mixer(h, hc, w_in, w_out, sink, rows, cols, with_ctx):
    def project(t):
        p = t @ w_in
        q, k, v = jnp.split(p, [C_WIDTH, C_WIDTH + C_KV_WIDTH], axis=-1)
        return split_heads(q, C_Q_HEADS), split_heads(k, C_KV_HEADS), split_heads(v, C_KV_HEADS)

    q, k, v = project(h)
    qc, kc, vc = project(hc)
    q = axial_rope(q, rows, cols)
    k = axial_rope(k, rows, cols)
    y = window_gqa_blocks(q, k, v, kc, vc, sink) @ w_out
    yc = None
    if with_ctx:
        yc = ctx_attention(qc, kc, vc, sink) @ w_out
    return y, yc

def swiglu(h, w_in, w_out):
    g, u = jnp.split(h @ w_in, 2, axis=-1)
    return (jax.nn.silu(g) * u) @ w_out

def first_inputs(seed: int = 0) -> dict:
    key = jax.random.key(seed)
    ks = jax.random.split(key, 24)
    D = D_MODEL

    def nrm(k, shape, std):
        return jax.random.normal(k, shape, dtype=jnp.float32) * std

    return {
        "x": nrm(ks[0], (BATCH, SEQ, D), 1.0),
        "c": nrm(ks[1], (BATCH, D), 1.0),
        "ctx": nrm(ks[2], (BATCH, CTX_LEN, D), 1.0),
        "c_ctx": nrm(ks[3], (D,), 1.0),
        "w_mod": nrm(ks[4], (DEPTH, D, 6 * D), 0.5 * D ** -0.5),
        "b_mod": nrm(ks[5], (DEPTH, 6 * D), 0.02),
        "g_pre_mix": 1.0 + nrm(ks[6], (DEPTH, D), 0.05),
        "g_post_mix": 1.0 + nrm(ks[7], (DEPTH, D), 0.05),
        "g_pre_ffn": 1.0 + nrm(ks[8], (DEPTH, D), 0.05),
        "g_post_ffn": 1.0 + nrm(ks[9], (DEPTH, D), 0.05),
        "we_in": nrm(ks[10], (N_EVEN, D, EVEN_IN), D ** -0.5),
        "we_out": nrm(ks[11], (N_EVEN, EVEN_MIX, D), EVEN_MIX ** -0.5),
        "we_q_gain": 1.0 + nrm(ks[12], (N_EVEN, HEAD_DIM), 0.05),
        "we_k_gain": 1.0 + nrm(ks[13], (N_EVEN, HEAD_DIM), 0.05),
        "we_pool": nrm(ks[14], (N_EVEN, B_GROUPS, B_GROUP_W, B_GROUP_W), B_GROUP_W ** -0.5),
        "we_pool_scale": 1.0 + nrm(ks[15], (N_EVEN, B_WIDTH), 0.1),
        "wo_in": nrm(ks[16], (N_ODD, D, ODD_IN), D ** -0.5),
        "wo_out": nrm(ks[17], (N_ODD, C_WIDTH, D), C_WIDTH ** -0.5),
        "wo_sink": nrm(ks[18], (N_ODD, C_Q_HEADS), 0.5),
        "w_ffn_in": nrm(ks[19], (DEPTH, D, 2 * FFN_HIDDEN), D ** -0.5),
        "w_ffn_out": nrm(ks[20], (DEPTH, FFN_HIDDEN, D), FFN_HIDDEN ** -0.5),
    }

def first_block(x, c, ctx, c_ctx, w_mod, b_mod, g_pre_mix, g_post_mix, g_pre_ffn, g_post_ffn,
              we_in, we_out, we_q_gain, we_k_gain, we_pool, we_pool_scale,
              wo_in, wo_out, wo_sink, w_ffn_in, w_ffn_out):
    S = x.shape[1]
    ROWS = S // GRID_W
    rows = jnp.repeat(jnp.arange(ROWS, dtype=jnp.int32), GRID_W)
    cols = jnp.tile(jnp.arange(GRID_W, dtype=jnp.int32), ROWS)
    silu_c = jax.nn.silu(c)
    silu_cc = jax.nn.silu(c_ctx)

    for l in range(DEPTH):
        with_ctx = l < DEPTH - 1
        mod = (silu_c @ w_mod[l] + b_mod[l])[:, None, :]
        mod_c = (silu_cc @ w_mod[l] + b_mod[l])[None, None, :]
        sh_m, sc_m, gt_m, sh_f, sc_f, gt_f = jnp.split(mod, 6, axis=-1)
        csh_m, csc_m, cgt_m, csh_f, csc_f, cgt_f = jnp.split(mod_c, 6, axis=-1)

        h = modulate(x, g_pre_mix[l], sh_m, sc_m)
        hc = modulate(ctx, g_pre_mix[l], csh_m, csc_m)
        i = l // 2
        if l % 2 == 0:
            y, yc = even_mixer(h, hc, we_in[i], we_out[i], we_q_gain[i], we_k_gain[i],
                               we_pool[i], we_pool_scale[i], rows, cols, with_ctx)
        else:
            y, yc = odd_mixer(h, hc, wo_in[i], wo_out[i], wo_sink[i], rows, cols, with_ctx)

        x = x + gt_m * rmsnorm(y, g_post_mix[l])
        h = modulate(x, g_pre_ffn[l], sh_f, sc_f)
        x = x + gt_f * rmsnorm(swiglu(h, w_ffn_in[l], w_ffn_out[l]), g_post_ffn[l])

        if with_ctx:
            ctx = ctx + cgt_m * rmsnorm(yc, g_post_mix[l])
            hc = modulate(ctx, g_pre_ffn[l], csh_f, csc_f)
            ctx = ctx + cgt_f * rmsnorm(swiglu(hc, w_ffn_in[l], w_ffn_out[l]), g_post_ffn[l])
    return x


NORM_EPS = 1e-6

A_HEADS = 8
A_NOPE = 64
A_ROPE = 32
A_KV_RANK = 128
A_V_DIM = 64
A_SCALE = (A_NOPE + A_ROPE) ** -0.5
IDX_HEADS = 8
IDX_DIM = 64
TOPK_MAX = 256

B_HEADS = 4
B_QK_DIM = 64
B_V_DIM = 2 * B_QK_DIM

C_HEADS = 16
C_GROUPS = 4
C_HPG = C_HEADS // C_GROUPS
C_DIM = 64
CMP_LEN = 32
CMP_STRIDE = 16
CMP_HIDDEN = 128
SEL_BLOCK = 64
SEL_TOPN = 16
WINDOW_2 = 512
C_Q_BLOCK = 16

D_FF = -(-8 * D_MODEL // (3 * 256)) * 256

EVEN_SPLITS = [A_HEADS * A_NOPE, A_HEADS * A_ROPE, A_KV_RANK, A_ROPE, IDX_HEADS * IDX_DIM, IDX_DIM, IDX_HEADS,
               B_HEADS * 2 * B_QK_DIM, B_HEADS * 2 * B_QK_DIM, B_HEADS * B_V_DIM]
EVEN_IN_2 = sum(EVEN_SPLITS)
ODD_SPLITS = [C_HEADS * C_DIM] + [C_GROUPS * C_DIM] * 6 + [C_HEADS * 3]
ODD_IN_2 = sum(ODD_SPLITS)


def rmsnorm_2(x, g):
    xf = x.astype(jnp.float32)
    y = xf * lax.rsqrt(jnp.mean(xf * xf, axis=-1, keepdims=True) + NORM_EPS)
    return (y * g.astype(jnp.float32)).astype(x.dtype)

def rope(x, pos):
    d = x.shape[-1]
    inv = ROPE_THETA ** (-jnp.arange(0, d, 2, dtype=jnp.float32) / d)
    ang = pos.astype(jnp.float32)[:, None] * inv[None, :]
    shape = (x.shape[1],) + (1,) * (x.ndim - 3) + (d // 2,)
    cos = jnp.cos(ang).reshape(shape)
    sin = jnp.sin(ang).reshape(shape)
    xf = x.astype(jnp.float32)
    x1, x2 = xf[..., :d // 2], xf[..., d // 2:]
    return jnp.concatenate([x1 * cos - x2 * sin, x2 * cos + x1 * sin], axis=-1).astype(x.dtype)

def safe_softmax(s, mask):
    s = jnp.where(mask, s, -jnp.inf)
    m = jnp.max(s, axis=-1, keepdims=True)
    m = jnp.where(jnp.isfinite(m), m, 0.0)
    e = jnp.exp(s - m)
    den = jnp.sum(e, axis=-1, keepdims=True)
    return e / jnp.where(den > 0, den, 1.0)

def split_cols(y, sizes):
    return jnp.split(y, np.cumsum(sizes)[:-1].tolist(), axis=-1)

def qslice(a, i, qb):
    return lax.dynamic_slice_in_dim(a, i * qb, qb, axis=1)

def map_blocks(fn, n_blocks):
    out = lax.map(fn, jnp.arange(n_blocks, dtype=jnp.int32))
    nb, b, qb = out.shape[:3]
    return jnp.moveaxis(out, 0, 1).reshape((b, nb * qb) + out.shape[3:])

def dsa_mixer(q_nope, q_rope, c_kv, k_rope, iq, ik, iw, kv_gain, w_uk, w_uv, pos):
    B, T = c_kv.shape[:2]
    q_nope = q_nope.reshape(B, T, A_HEADS, A_NOPE)
    q_rope = rope(q_rope.reshape(B, T, A_HEADS, A_ROPE), pos)
    c_kv = rmsnorm_2(c_kv, kv_gain)
    k_rope = rope(k_rope, pos)
    q_lat = jnp.einsum('bthd,hdc->bthc', q_nope, w_uk)
    qc = jnp.concatenate([q_lat, q_rope], axis=-1)
    kc = jnp.concatenate([c_kv, k_rope], axis=-1)
    iq = rope(iq.reshape(B, T, IDX_HEADS, IDX_DIM), pos)
    ik = rope(ik, pos)
    iw = iw * IDX_HEADS ** -0.5
    k_sel = min(TOPK_MAX, T // 4)

    def block(i):
        t = i * Q_BLOCK + jnp.arange(Q_BLOCK, dtype=jnp.int32)
        rel = jax.nn.relu(jnp.einsum('bqhd,bsd->bqhs', qslice(iq, i, Q_BLOCK), ik).astype(jnp.float32) * IDX_DIM ** -0.5)
        score = jnp.einsum('bqhs,bqh->bqs', rel, qslice(iw, i, Q_BLOCK).astype(jnp.float32))
        causal = pos[None, :] <= t[:, None]
        score = jnp.where(causal[None], score, -jnp.inf)
        _, idx = lax.top_k(score, k_sel)
        kg = jax.vmap(lambda k, j: k[j])(kc, idx)
        s = jnp.einsum('bqhc,bqkc->bqhk', qslice(qc, i, Q_BLOCK), kg).astype(jnp.float32) * A_SCALE
        valid = (idx <= t[None, :, None])[:, :, None, :]
        p = safe_softmax(s, valid)
        return jnp.einsum('bqhk,bqkc->bqhc', p.astype(kg.dtype), kg[..., :A_KV_RANK])

    o_lat = map_blocks(block, T // Q_BLOCK)
    o = jnp.einsum('bthc,hcd->bthd', o_lat, w_uv)
    return o.reshape(B, T, A_HEADS * A_V_DIM)

def diff_mixer(q, k, v, lam, subln_gain, lam_init, pos):
    B, T = q.shape[:2]
    q = rope(q.reshape(B, T, B_HEADS * 2, B_QK_DIM), pos).reshape(B, T, B_HEADS, 2, B_QK_DIM)
    k = rope(k.reshape(B, T, B_HEADS * 2, B_QK_DIM), pos).reshape(B, T, B_HEADS, 2, B_QK_DIM)
    v = v.reshape(B, T, B_HEADS, B_V_DIM)
    lf = lam.astype(jnp.float32)
    lam_full = jnp.exp(jnp.sum(lf[0] * lf[1])) - jnp.exp(jnp.sum(lf[2] * lf[3])) + lam_init

    def block(i):
        t = i * Q_BLOCK + jnp.arange(Q_BLOCK, dtype=jnp.int32)
        s = jnp.einsum('bqhmd,bshmd->bhmqs', qslice(q, i, Q_BLOCK), k).astype(jnp.float32) * B_QK_DIM ** -0.5
        causal = pos[None, :] <= t[:, None]
        p = safe_softmax(s, causal)
        a = p[:, :, 0] - lam_full * p[:, :, 1]
        return jnp.einsum('bhqs,bshe->bqhe', a.astype(v.dtype), v)

    o = map_blocks(block, T // Q_BLOCK)
    o = rmsnorm_2(o, subln_gain) * (1.0 - lam_init)
    return o.reshape(B, T, B_HEADS * B_V_DIM)

def compress(x, pe, w1, w2):
    B, T, G, d = x.shape
    chunks = x.reshape(B, T // CMP_STRIDE, CMP_STRIDE, G, d)
    blocks = jnp.concatenate([chunks[:, :-1], chunks[:, 1:]], axis=2) + pe[None, None, :, None, :]
    flat = blocks.transpose(0, 1, 3, 2, 4).reshape(B, -1, G, CMP_LEN * d)
    return jnp.einsum('bngf,fe->bnge', jax.nn.gelu(flat @ w1), w2)

def nsa_mixer(q, kc_raw, vc_raw, ks, vs, kw, vw, gates, pe, w1, w2, pos):
    B, T = q.shape[:2]
    kv = lambda a: a.reshape(B, T, C_GROUPS, C_DIM)
    q = rope(q.reshape(B, T, C_HEADS, C_DIM), pos).reshape(B, T, C_GROUPS, C_HPG, C_DIM)
    k_cmp = compress(rope(kv(kc_raw), pos), pe[0], w1[0], w2[0])
    v_cmp = compress(kv(vc_raw), pe[1], w1[1], w2[1])
    k_slc, v_slc = rope(kv(ks), pos), kv(vs)
    k_win, v_win = rope(kv(kw), pos), kv(vw)
    gates = jax.nn.sigmoid(gates.astype(jnp.float32)).reshape(B, T, C_GROUPS, C_HPG, 3).astype(q.dtype)
    n_cmp = T // CMP_STRIDE - 1
    n_blk = T // SEL_BLOCK
    top_n = min(SEL_TOPN, n_blk)
    cmp_end = jnp.arange(n_cmp, dtype=jnp.int32) * CMP_STRIDE + CMP_LEN - 1
    cs = np.arange(n_cmp) * CMP_STRIDE
    ss = np.arange(n_blk) * SEL_BLOCK
    overlap = jnp.asarray(((cs[:, None] < ss[None, :] + SEL_BLOCK) & (cs[:, None] + CMP_LEN > ss[None, :])).astype(np.float32))
    k_blocks = k_slc.reshape(B, n_blk, SEL_BLOCK, C_GROUPS, C_DIM).transpose(0, 3, 1, 2, 4)
    v_blocks = v_slc.reshape(B, n_blk, SEL_BLOCK, C_GROUPS, C_DIM).transpose(0, 3, 1, 2, 4)
    k_pad = jnp.pad(k_win, ((0, 0), (WINDOW_2, 0), (0, 0), (0, 0)))
    v_pad = jnp.pad(v_win, ((0, 0), (WINDOW_2, 0), (0, 0), (0, 0)))
    blk_ids = jnp.arange(n_blk, dtype=jnp.int32)
    scale = C_DIM ** -0.5
    gather = jax.vmap(jax.vmap(lambda a, j: a[j]))

    def block(i):
        t = i * C_Q_BLOCK + jnp.arange(C_Q_BLOCK, dtype=jnp.int32)
        qb = qslice(q, i, C_Q_BLOCK)
        s = jnp.einsum('bqghd,bngd->bqghn', qb, k_cmp).astype(jnp.float32) * scale
        p_cmp = safe_softmax(s, (cmp_end[None, :] <= t[:, None])[:, None, None, :])
        o_cmp = jnp.einsum('bqghn,bngd->bqghd', p_cmp.astype(v_cmp.dtype), v_cmp)
        imp = jnp.einsum('bqghn,nj->bqgj', p_cmp, overlap)
        cur = t // SEL_BLOCK
        forced = (blk_ids[None, :] == 0) | (blk_ids[None, :] == cur[:, None]) | (blk_ids[None, :] == cur[:, None] - 1)
        admissible = blk_ids[None, :] * SEL_BLOCK <= t[:, None]
        imp = jnp.where(forced[:, None, :], jnp.inf, imp)
        imp = jnp.where(admissible[:, None, :], imp, -jnp.inf)
        _, sel = lax.top_k(imp, top_n)
        sel = sel.transpose(0, 2, 1, 3)
        kg = gather(k_blocks, sel)
        vg = gather(v_blocks, sel)
        s = jnp.einsum('bqghd,bgqnld->bqghnl', qb, kg).astype(jnp.float32) * scale
        tok = sel[..., None] * SEL_BLOCK + jnp.arange(SEL_BLOCK, dtype=jnp.int32)
        m_slc = (tok <= t[None, None, :, None, None]).transpose(0, 2, 1, 3, 4)
        m_slc = m_slc.reshape(B, C_Q_BLOCK, C_GROUPS, 1, top_n * SEL_BLOCK)
        p = safe_softmax(s.reshape(B, C_Q_BLOCK, C_GROUPS, C_HPG, top_n * SEL_BLOCK), m_slc)
        p = p.reshape(B, C_Q_BLOCK, C_GROUPS, C_HPG, top_n, SEL_BLOCK)
        o_slc = jnp.einsum('bqghnl,bgqnld->bqghd', p.astype(vg.dtype), vg)
        kwb = lax.dynamic_slice_in_dim(k_pad, i * C_Q_BLOCK, WINDOW_2 + C_Q_BLOCK, axis=1)
        vwb = lax.dynamic_slice_in_dim(v_pad, i * C_Q_BLOCK, WINDOW_2 + C_Q_BLOCK, axis=1)
        kpos = i * C_Q_BLOCK - WINDOW_2 + jnp.arange(WINDOW_2 + C_Q_BLOCK, dtype=jnp.int32)
        dist = t[:, None] - kpos[None, :]
        m_win = ((dist >= 0) & (dist < WINDOW_2) & (kpos[None, :] >= 0))[:, None, None, :]
        s = jnp.einsum('bqghd,bsgd->bqghs', qb, kwb).astype(jnp.float32) * scale
        p = safe_softmax(s, m_win)
        o_win = jnp.einsum('bqghs,bsgd->bqghd', p.astype(vwb.dtype), vwb)
        g = qslice(gates, i, C_Q_BLOCK)
        return g[..., 0:1] * o_cmp + g[..., 1:2] * o_slc + g[..., 2:3] * o_win

    o = map_blocks(block, T // C_Q_BLOCK)
    return o.reshape(B, T, C_HEADS * C_DIM)

def swiglu_2(h, w_gate, w_up, w_down):
    return (jax.nn.silu(h @ w_gate) * (h @ w_up)) @ w_down

def _w(key, shape, fan_in, gain=1.0):
    return jax.random.normal(key, shape, jnp.float32) * (gain * fan_in ** -0.5)

def _gain(key, shape):
    return 1.0 + 0.02 * jax.random.normal(key, shape, jnp.float32)

def second_inputs(seed: int = 0) -> dict:
    key = jax.random.key(seed)
    k = jax.random.split(key, 19)
    n_even = (DEPTH + 1) // 2
    n_odd = DEPTH // 2
    out_gain = (2 * DEPTH) ** -0.5
    return {
        'x': jax.random.normal(k[0], (BATCH, SEQ, D_MODEL), jnp.float32),
        'norm_mix': _gain(k[1], (DEPTH, D_MODEL)),
        'norm_ffn': _gain(k[2], (DEPTH, D_MODEL)),
        'norm_final': _gain(k[3], (D_MODEL,)),
        'ev_w_in': _w(k[4], (n_even, D_MODEL, EVEN_IN_2), D_MODEL),
        'ev_kv_gain': _gain(k[5], (n_even, A_KV_RANK)),
        'ev_w_uk': _w(k[6], (n_even, A_HEADS, A_NOPE, A_KV_RANK), A_KV_RANK),
        'ev_w_uv': _w(k[7], (n_even, A_HEADS, A_KV_RANK, A_V_DIM), A_KV_RANK),
        'ev_lambda': 0.1 * jax.random.normal(k[8], (n_even, 4, B_QK_DIM), jnp.float32),
        'ev_subln': _gain(k[9], (n_even, B_V_DIM)),
        'ev_w_out': _w(k[10], (n_even, D_MODEL, D_MODEL), D_MODEL, out_gain),
        'od_w_in': _w(k[11], (n_odd, D_MODEL, ODD_IN_2), D_MODEL),
        'od_cmp_pe': 0.1 * jax.random.normal(k[12], (n_odd, 2, CMP_LEN, C_DIM), jnp.float32),
        'od_cmp_w1': _w(k[13], (n_odd, 2, CMP_LEN * C_DIM, CMP_HIDDEN), CMP_LEN * C_DIM),
        'od_cmp_w2': _w(k[14], (n_odd, 2, CMP_HIDDEN, C_DIM), CMP_HIDDEN),
        'od_w_out': _w(k[15], (n_odd, D_MODEL, D_MODEL), D_MODEL, out_gain),
        'ffn_w_gate': _w(k[16], (DEPTH, D_MODEL, D_FF), D_MODEL),
        'ffn_w_up': _w(k[17], (DEPTH, D_MODEL, D_FF), D_MODEL),
        'ffn_w_down': _w(k[18], (DEPTH, D_FF, D_MODEL), D_FF, out_gain),
    }

def second_block(x, norm_mix, norm_ffn, norm_final,
              ev_w_in, ev_kv_gain, ev_w_uk, ev_w_uv, ev_lambda, ev_subln, ev_w_out,
              od_w_in, od_cmp_pe, od_cmp_w1, od_cmp_w2, od_w_out,
              ffn_w_gate, ffn_w_up, ffn_w_down):
    pos = jnp.arange(x.shape[1], dtype=jnp.int32)
    for layer in range(DEPTH):
        j = layer // 2
        h = rmsnorm_2(x, norm_mix[layer])
        if layer % 2 == 0:
            y = h @ ev_w_in[j]
            qa_nope, qa_rope, c_kv, ka_rope, iq, ik, iw, qb, kb, vb = split_cols(y, EVEN_SPLITS)
            o_a = dsa_mixer(qa_nope, qa_rope, c_kv, ka_rope, iq, ik, iw, ev_kv_gain[j], ev_w_uk[j], ev_w_uv[j], pos)
            lam_init = 0.8 - 0.6 * math.exp(-0.3 * layer)
            o_b = diff_mixer(qb, kb, vb, ev_lambda[j], ev_subln[j], lam_init, pos)
            mix = jnp.concatenate([o_a, o_b], axis=-1) @ ev_w_out[j]
        else:
            y = h @ od_w_in[j]
            qc, kc_raw, vc_raw, ks, vs, kw, vw, gc = split_cols(y, ODD_SPLITS)
            o_c = nsa_mixer(qc, kc_raw, vc_raw, ks, vs, kw, vw, gc, od_cmp_pe[j], od_cmp_w1[j], od_cmp_w2[j], pos)
            mix = o_c @ od_w_out[j]
        x = x + mix
        x = x + swiglu_2(rmsnorm_2(x, norm_ffn[layer]), ffn_w_gate[layer], ffn_w_up[layer], ffn_w_down[layer])
    return rmsnorm_2(x, norm_final)


def setup_inputs(seed=0):
    out = dict(first_inputs(seed))
    for name, value in second_inputs(seed + 1).items():
        if name != "x":
            out[name + "_2"] = value
    return out


def reference(
    x, c, ctx, c_ctx, w_mod, b_mod, g_pre_mix, g_post_mix, g_pre_ffn, g_post_ffn, we_in, we_out,
    we_q_gain, we_k_gain, we_pool, we_pool_scale, wo_in, wo_out, wo_sink, w_ffn_in, w_ffn_out,
    norm_mix_2, norm_ffn_2, norm_final_2, ev_w_in_2, ev_kv_gain_2, ev_w_uk_2, ev_w_uv_2,
    ev_lambda_2, ev_subln_2, ev_w_out_2, od_w_in_2, od_cmp_pe_2, od_cmp_w1_2, od_cmp_w2_2,
    od_w_out_2, ffn_w_gate_2, ffn_w_up_2, ffn_w_down_2,
):
    x = first_block(
        x, c, ctx, c_ctx, w_mod, b_mod, g_pre_mix, g_post_mix, g_pre_ffn, g_post_ffn, we_in,
        we_out, we_q_gain, we_k_gain, we_pool, we_pool_scale, wo_in, wo_out, wo_sink, w_ffn_in,
        w_ffn_out,
    )
    return second_block(
        x, norm_mix_2, norm_ffn_2, norm_final_2, ev_w_in_2, ev_kv_gain_2, ev_w_uk_2, ev_w_uv_2,
        ev_lambda_2, ev_subln_2, ev_w_out_2, od_w_in_2, od_cmp_pe_2, od_cmp_w1_2, od_cmp_w2_2,
        od_w_out_2, ffn_w_gate_2, ffn_w_up_2, ffn_w_down_2,
    )


_drawn_inputs = setup_inputs


def setup_inputs(seed=0):
    import zlib

    import numpy as np

    out = dict(_drawn_inputs(seed))
    spreads = {}
    factors = {'g_pre_mix': 2.685,
     'we_q_gain': 8.0,
     'we_k_gain': 8.0,
     'wo_sink': 64.0,
     'norm_mix_2': 6.447,
     'norm_ffn_2': 6.014,
     'norm_final_2': 8.096,
     'ev_kv_gain_2': 8.0,
     'ev_lambda_2': 7.579,
     'ev_subln_2': 8.0,
     'od_cmp_pe_2': 4.639}
    for name, (base, spread) in spreads.items():
        noise = np.random.default_rng([zlib.crc32(name.encode()), seed]).standard_normal(out[name].shape)
        drawn = base * np.exp(spread * noise) if base else spread * noise
        out[name] = __import__('jax').numpy.asarray(drawn.astype(out[name].dtype))
    for name, factor in factors.items():
        out[name] = (out[name] * factor).astype(out[name].dtype)
    return out
```

```python
import math
from contextlib import ExitStack, contextmanager

import numpy as np

import concourse.bass as bass
from concourse import mybir

F32 = mybir.dt.float32
F32R = mybir.dt.float32r
BF16 = mybir.dt.bfloat16
ALU = mybir.AluOpType
ACT = mybir.ActivationFunctionType
AX = mybir.AxisListType

P = 128
D = 1024
DC = D // P
SEQ = 512
CTX = 256
TOK = SEQ + CTX
QT = SEQ // P
HD = 64
FFN = 2816
FC = FFN // P
KMAX = 8
EPS = 1e-6
NEG = -1e30
TAKEN = -3e38
TOPK = 128
CMP_N = 31
CMP_LEN = 32
CMP_STRIDE = 16
X_ONLY = [(0, SEQ)]
X_CTX = [(0, SEQ), (SEQ, TOK)]
FFN_CHUNKS = [(0, 8), (8, 16), (16, 22)]
WINDOWS = (2, 4, 8, 16)
LAM_INIT = 0.8 - 0.6 * math.exp(0.0)
A_SCALE = 96.0 ** -0.5


class Chain:

    def __init__(self, eng, sem):
        self.eng, self.sem, self.n, self.i, self.per, self.base = eng, sem, 0, None, 0, 0

    def value(self):
        return self.n if self.i is None else self.i * self.per + self.base + self.n

    def mark(self, ins):
        ins.then_inc(self.sem, 1)
        self.n += 1
        return self.value()

    def link(self, ins):
        self.eng.wait_ge(self.sem, self.mark(ins))

    @contextmanager
    def loop(self, count, per):
        if count == 1:
            n = self.n
            yield 0
            assert self.n - n == per, (self.n - n, per)
            return
        with self.eng.Fori(0, count) as i:
            self.i, self.per, self.base, self.n = i, per, self.n, 0
            yield i
            assert self.n == per, (self.n, per)
        self.n, self.i = self.base + count * per, None


class Kit:

    def __init__(self, nc, ctx):
        self.nc, self.ctx, self.total = nc, ctx, {}
        self.sems = {}
        self.counted = []
        self.slab_count = 0
        self.side_in = 0
        self.base0 = -(-nc.sbuf_base // 64) * 64
        self.stages = []

    def sem(self, name):
        if name not in self.sems:
            self.sems[name] = self.ctx.enter_context(self.nc.semaphore(name))
            self.total[name] = 0
        return self.sems[name]

    def reserve(self, name, n):
        self.sem(name)
        if name not in self.counted:
            self.counted.append(name)
            self.total[name] = 1
        base = self.total[name]
        self.total[name] = base + n
        return base

    def dma_count(self, name, n):
        self.sem(name)
        base = self.total[name]
        self.total[name] = base + 16 * n
        return base

    def at(self, name, shape, dt, offset):
        return self.nc.alloc_sbuf_tensor_at(name, shape, dt, offset=self.base0 + offset)


def flat(ap):
    return ap.rearrange("p a b -> p (a b)")


class Stage:
    def __init__(self, kit):
        self.kit = kit
        self.number = len(kit.stages)
        kit.stages.append(self)

    def enter(self, eng):
        for name in ("pe", "act", "dve", "pool"):
            eng.wait_ge(self.kit.sem("met_" + name), self.number)

    def sync(self, sp):
        pass

    def tensor(self, pe):
        pass

    def vector(self, dve, chain):
        pass

    def scalar(self, act, chain):
        pass

    def gpsimd(self, pool, chain):
        pass


class Start(Stage):

    def __init__(self, kit, loads):
        super().__init__(kit)
        self.loads = loads
        self.s = kit.sem("loaded")
        kit.reserve("w_lo_ready", 2)
        kit.reserve("idx_relu", 4)
        kit.reserve("idx_acc", 2)
        kit.reserve("slab_mm", 2)
        kit.reserve("psum_free0", 1)
        kit.reserve("psum_free1", 1)
        kit.reserve("o_free", 2)

    def sync(self, sp):
        for dst, src in self.loads:
            sp.dma_start(dst, src).then_inc(self.s, 16)

    def gpsimd(self, pool, chain):
        k = self.kit
        ahead = {"w_lo_ready": 2, "idx_relu": 4, "idx_acc": 2, "slab_mm": 2, "psum_free0": 1, "psum_free1": 1, "o_free": 2}
        for name in k.counted:
            pool.sem_inc(k.sems[name], 1 + ahead.get(name, 0))
        pool.wait_ge(self.s, 16 * len(self.loads))


class Modulation(Stage):
    TURN_PE, TURN_BOTH, TURN_X = 5, 3, 4

    def __init__(self, kit, w, w_rows):
        super().__init__(kit)
        self.w, self.w_rows = w, w_rows
        self.rows = self.TURN_BOTH + self.TURN_X
        self.n = w.shape[0] // self.TURN_PE
        assert w_rows.shape[0] == self.rows * self.n
        for r in range(self.TURN_PE):
            kit.sem(f"mod_in{r}")
            kit.reserve(f"mod_free{r}", self.n)
            kit.reserve(f"mod_taken{r}", self.n)
        for r in range(self.rows):
            kit.sem(f"row_in{r}")
            kit.reserve(f"row_free{r}", self.n)
        kit.sem("silu_c")

    def sync(self, sp):
        k = self.kit

        def rows(i, q):
            sp.wait_ge(k.sems[f"row_free{q}"], i + 1)
            sp.dma_start(k.row_ring[:, q], self.w_rows[bass.ds(i * self.rows + q, 1)].rearrange("o p n -> p (o n)")).then_inc(k.sems[f"row_in{q}"], 16)

        with sp.Fori(0, self.n) as i:
            for r in range(self.TURN_PE):
                sp.wait_ge(k.sems[f"mod_free{r}"], i + 1)
                sp.dma_start(k.mod_ring[:, r], self.w[bass.ds(i * self.TURN_PE + r, 1)].rearrange("o p n -> p (o n)")).then_inc(k.sems[f"mod_in{r}"], 16)
                rows(i, r)
            for q in range(self.TURN_PE, self.rows):
                rows(i, q)

    def scalar(self, act, chain):
        k = self.kit
        act.activation(k.c_all[:], k.c_all[:], ACT.Silu)
        act.activation(k.silu_c[:], k.c_cols[:], ACT.Silu)
        act.drain().then_inc(k.sems["silu_c"], 1)

    def tensor(self, pe):
        k = self.kit
        pe.wait_ge(k.sems["silu_c"], 1)
        with pe.Fori(0, self.n) as i:
            for r in range(self.TURN_PE):
                pe.wait_ge(k.sems[f"mod_taken{r}"], i + 1)
                pe.wait_ge(k.sems[f"mod_in{r}"], i * 16 + 16)
                for s in range(2):
                    for c in range(DC):
                        last = pe.matmul(k.ps[:, r, 2 * s:2 * s + 2],
                                         k.mod_ring[:, r, (s * DC + c) * P:(s * DC + c + 1) * P],
                                         k.silu_c[:, c, :], start=(c == 0), stop=(c == DC - 1))
                last.then_inc(k.sems[f"mod_free{r}"], 1)

    def vector(self, dve, chain):
        k = self.kit
        first_row = 2 * self.TURN_PE * self.n
        first_x = first_row + 2 * self.TURN_BOTH * self.n
        dve.wait_ge(k.sems["silu_c"], 1)
        with chain.loop(self.n, 4 * self.TURN_BOTH + 2 * self.TURN_X) as i:
            done = []

            def rows(q):
                dve.wait_ge(k.sems[f"row_in{q}"], i * 16 + 16)
                both = q < self.TURN_BOTH
                for t in range(2):
                    tile = i * (2 * self.TURN_BOTH) + (first_row + 2 * q + t) if both else i * (2 * self.TURN_X) + (first_x + 2 * (q - self.TURN_BOTH) + t)
                    for j in range(2 if both else 1):
                        m = len(done)
                        if m >= 4:
                            dve.wait_ge(chain.sem, done[m - 4])
                        ins = dve.scalar_tensor_tensor(k.row_out[:, m % 4, :], k.row_ring[:, q, t * D:(t + 1) * D], 1.0, k.c_all[:, j, :], ALU.mult, ALU.mult,
                                                       accum_out=k.modv[:, bass.ds(tile, 1), j])
                        done.append(chain.mark(ins))
                dve.wait_ge(chain.sem, done[-1])
                dve.sem_inc(k.sems[f"row_free{q}"], 1)

            for r in range(self.TURN_PE):
                rows(r)
                dve.wait_ge(k.sems[f"mod_free{r}"], i + 2)
                at = bass.ds(i * (2 * self.TURN_PE) + 2 * r, 2)
                dve.tensor_tensor(k.modv[:, at, :], k.ps[:, r, 0:4].rearrange("p (n j) -> p n j", j=2),
                                  k.b_mod[:, at].unsqueeze(2).to_broadcast([P, 2, 2]), ALU.add).then_inc(k.sems[f"mod_taken{r}"], 1)
            for q in range(self.TURN_PE, self.rows):
                rows(q)
        for r in range(self.TURN_PE):
            dve.wait_ge(k.sems[f"mod_taken{r}"], self.n + 1)
        dve.tensor_tensor(k.modv[:, first_row:, 0], k.modv[:, first_row:, 0], k.b_mod[:, first_row:], ALU.add)
        chain.link(dve.tensor_tensor(k.modv[:, first_row:first_x, 1], k.modv[:, first_row:first_x, 1], k.b_mod[:, first_row:first_x], ALU.add))
        for l in range(2):
            for j in range(2):
                v = lambda part: k.modv[:, (l * 6 + part) * DC:(l * 6 + part + 1) * DC, j]
                g = lambda t: k.gains[:, t, l * DC:(l + 1) * DC]
                chain.link(dve.scalar_tensor_tensor(k.scale_mix[:, l, j], v(1), 1.0, g(0), ALU.add, ALU.mult))
                dve.tensor_copy(k.shift_mix[:, l, j], v(0))
                if l == 1 and j == 1:
                    continue
                dve.scalar_tensor_tensor(k.scale_ffn[:, l, j], v(4), 1.0, g(2), ALU.add, ALU.mult)
                dve.tensor_tensor(k.gate_mix[:, l, j], v(2), g(1), ALU.mult)
                dve.tensor_tensor(k.gate_ffn[:, l, j], v(5), g(3), ALU.mult)
                chain.link(dve.tensor_copy(k.shift_ffn[:, l, j], v(3)))


class Norm(Stage):

    def __init__(self, kit, kind, src, groups, cols, shift=None, dst=None):
        super().__init__(kit)
        self.kind, self.src, self.groups, self.cols, self.shift, self.dst = kind, src, groups, cols, shift, dst
        self.T = groups[-1][1]
        self.b = {n: kit.reserve(n, c) for n, c in (
            ("sq_ready", DC), ("sq_used", DC), ("sums_ready", 1), ("std_ready", 1), ("rstd_ready", 1),
            ("norm_t", DC * (kind == "split")), ("norm_hi", DC * (kind == "split")), ("norm_lo", DC * (kind == "split")))}

    def scalar(self, act, chain):
        k, b, T = self.kit, self.b, self.T
        for c in range(DC):
            if c >= 2:
                act.wait_ge(k.sems["sq_used"], b["sq_used"] + c - 1)
            act.activation(k.n_sq[:, c % 2, :T], self.src[:, c, :T], ACT.Square).then_inc(k.sems["sq_ready"], 1)
        act.wait_ge(k.sems["sums_ready"], b["sums_ready"] + 1)
        act.activation(k.n_rs[:, :T], flat(k.ps[:, 0:2])[:, :T], ACT.Sqrt, bias=k.eps[:, 0:1], scale=1.0 / D).then_inc(k.sems["std_ready"], 1)
        if self.kind != "split":
            return
        for c in range(DC):
            act.wait_ge(k.sems["norm_t"], b["norm_t"] + c + 1)
            if c >= 2:
                act.wait_ge(k.sems["norm_lo"], b["norm_lo"] + c - 1)
            for j, (t0, t1) in enumerate(self.groups):
                ins = act.activation(k.n_h[:, c % 2, t0:t1], k.n_t[:, c % 2, t0:t1], ACT.Identity,
                                     bias=self.shift[:, j, c:c + 1] if self.shift is not None else 0.0,
                                     scale=self.cols[:, j, c:c + 1])
            chain.link(ins)
            act.activation(k.h_hi[:, c, :T], k.n_h[:, c % 2, :T], ACT.Copy).then_inc(k.sems["norm_hi"], 1)

    def tensor(self, pe):
        k, b, T = self.kit, self.b, self.T
        for c in range(DC):
            pe.wait_ge(k.sems["sq_ready"], b["sq_ready"] + c + 1)
            for g, (t0, t1) in enumerate(self.groups):
                ins = pe.matmul(k.ps[:, g, 0:t1 - t0], k.ones[:], k.n_sq[:, c % 2, t0:t1], start=(c == 0), stop=(c == DC - 1))
            ins.then_inc(k.sems["sq_used"], 1)
        pe.drain().then_inc(k.sems["sums_ready"], 1)

    def vector(self, dve, chain):
        k, b, T = self.kit, self.b, self.T
        dve.wait_ge(k.sems["std_ready"], b["std_ready"] + 1)
        chain.link(dve.reciprocal(k.n_r[:, :T], k.n_rs[:, :T]))
        if self.kind == "split":
            for c in range(DC + 1):
                if c < DC:
                    if c >= 2:
                        dve.wait_ge(k.sems["norm_hi"], b["norm_hi"] + c - 1)
                    dve.tensor_tensor(k.n_t[:, c % 2, :T], self.src[:, c, :T], k.n_r[:, :T], ALU.mult).then_inc(k.sems["norm_t"], 1)
                if c >= 1:
                    dve.wait_ge(k.sems["norm_hi"], b["norm_hi"] + c)
                    dve.tensor_tensor(k.h_lo[:, c - 1, :T], k.n_h[:, (c - 1) % 2, :T], k.h_hi[:, c - 1, :T].bitcast(F32), ALU.subtract).then_inc(k.sems["norm_lo"], 1)
        else:
            for c in range(DC):
                v = chain.mark(dve.tensor_tensor(k.n_t[:, c % 2, :T], self.src[:, c, :T], k.n_r[:, :T], ALU.mult))
                dve.wait_ge(chain.sem, v)
                for j, (t0, t1) in enumerate(self.groups):
                    if self.kind == "gate":
                        ins = dve.scalar_tensor_tensor(k.x[:, c, t0:t1], k.n_t[:, c % 2, t0:t1], self.cols[:, j, c:c + 1], k.x[:, c, t0:t1], ALU.mult, ALU.add)
                    else:
                        ins = dve.tensor_scalar(self.dst[:, c, t0:t1], k.n_t[:, c % 2, t0:t1], self.cols[:, j, c:c + 1], None, ALU.mult)


class Linear(Stage):

    def __init__(self, kit, w, hi, lo, groups, mode, dst=None, segs=None):
        super().__init__(kit)
        self.w, self.hi, self.lo, self.groups, self.mode, self.dst = w, hi, lo, groups, mode, dst
        self.M, self.KT, self.T = w.shape[0], w.shape[2] // P, groups[-1][1]
        self.segs = segs or [(0, self.M, 1.0)]
        M = self.M
        self.n0 = kit.slab_count
        kit.slab_count += M
        self.b_hi = kit.reserve("w_hi_ready", M)
        self.b_lo = kit.reserve("w_lo_ready", M)
        self.b_mm = kit.reserve("slab_mm", M)
        for e in range(2):
            kit.reserve(f"psum_free{e}", (M + 1) // 2 if self.slot(0) == e else M // 2)
            kit.sem(f"raw_in{e}")
        self.b_silu = kit.reserve("silu_ready", M // 2 if mode == "gated" else 0)
        self.b_su = kit.reserve("silu_used", M // 2 if mode == "gated" else 0)

    def slot(self, e):
        return (self.n0 + e) % 2

    def slabs(self, eng, body, m0=0, m1=None):
        m1 = self.M if m1 is None else m1
        n = (m1 - m0) // 2
        if n > 1:
            with eng.Fori(0, n) as i:
                for e in range(2):
                    body(i * 2 + (m0 + e), i, m0 + e)
        elif n == 1:
            for e in range(2):
                body(m0 + e, 0, m0 + e)
        if (m1 - m0) % 2:
            body(m1 - 1, n, m0)

    def turn(self, i, e):
        return i + (self.n0 + e) // 2

    def sync(self, sp):
        k = self.kit

        def load(m, i, e):
            s = self.slot(e)
            sp.wait_ge(k.sems["w_lo_ready"], m + (self.b_lo - 1))
            sp.dma_start(k.w_raw[:, s, 0:self.KT * P], (self.w[bass.ds(m, 1)] if not isinstance(m, int) else self.w[m:m + 1]).rearrange("o p n -> p (o n)")).then_inc(k.sems[f"raw_in{s}"], 16)

        self.slabs(sp, load)

    def high(self, act, m, i, e):
        k, s = self.kit, self.slot(e)
        act.wait_ge(k.sems[f"raw_in{s}"], self.turn(i, e) * 16 + 16)
        act.wait_ge(k.sems["slab_mm"], m + (self.b_mm - 1))
        act.activation(k.w_hi[:, s, 0:self.KT * P], k.w_raw[:, s, 0:self.KT * P], ACT.Copy).then_inc(k.sems["w_hi_ready"], 1)

    def scalar(self, act, chain):
        k = self.kit
        if self.mode != "gated":
            self.slabs(act, lambda m, i, e: self.high(act, m, i, e))
            return
        pairs, T = self.M // 2, self.T

        def silu(p, i):
            s = self.slot(0)
            act.wait_ge(k.sems["slab_mm"], p * 2 + (self.b_mm + 1))
            act.wait_ge(k.sems["silu_used"], p + self.b_su)
            ins = act.activation(k.f_s[:, :T], flat(k.ps[:, 2 * s:2 * s + 2])[:, :T], ACT.Silu)
            chain.link(ins)
            act.sem_inc(k.sems["silu_ready"], 1)
            act.sem_inc(k.sems[f"psum_free{s}"], 1)

        self.high(act, 0, 0, 0)
        self.high(act, 1, 0, 1)
        with chain.loop(pairs - 1, 1) as i:
            self.high(act, i * 2 + 2, i, 2)
            silu(i, i)
            self.high(act, i * 2 + 3, i, 3)
        silu(pairs - 1, pairs - 1)

    def gpsimd(self, pool, chain):
        k = self.kit

        def low(m, i, e):
            s = self.slot(e)
            pool.wait_ge(k.sems["w_hi_ready"], m + (self.b_hi + 1))
            ins = pool.tensor_tensor(k.w_lo[:, s, 0:self.KT * P], k.w_raw[:, s, 0:self.KT * P], k.w_hi[:, s, 0:self.KT * P].bitcast(F32), ALU.subtract)
            ins.then_inc(k.sems["w_lo_ready"], 1)

        self.slabs(pool, low)

    def tensor(self, pe):
        k = self.kit

        def tile(m, i, e):
            s = self.slot(e)
            pe.wait_ge(k.sems["w_hi_ready"], m + (self.b_hi + 1))
            pe.wait_ge(k.sems[f"psum_free{s}"], self.turn(i, e) + 2)
            for n, (w, h) in enumerate(((k.w_hi, self.hi), (k.w_hi, self.lo), (k.w_lo, self.hi))):
                if n == 2:
                    pe.wait_ge(k.sems["w_lo_ready"], m + (self.b_lo + 1))
                for c in range(self.KT):
                    for g, (t0, t1) in enumerate(self.groups):
                        ins = pe.matmul(k.ps[:, 2 * s + g, 0:t1 - t0], w[:, s, c * P:(c + 1) * P], h[:, c, t0:t1],
                                        start=(n == 0 and c == 0), stop=(n == 2 and c == self.KT - 1))
            ins.then_inc(k.sems["slab_mm"], 1)

        self.slabs(pe, tile)

    def vector(self, dve, chain):
        k, T = self.kit, self.T
        if self.mode == "gated":
            s = self.slot(1)
            with chain.loop(self.M // 2, 3) as p:
                dve.wait_ge(k.sems["silu_ready"], p + (self.b_silu + 1))
                dve.wait_ge(k.sems["slab_mm"], p * 2 + (self.b_mm + 2))
                chain.link(dve.tensor_tensor(k.f_t[:, :T], k.f_s[:, :T], flat(k.ps[:, 2 * s:2 * s + 2])[:, :T], ALU.mult))
                dve.sem_inc(k.sems[f"psum_free{s}"], 1)
                dve.sem_inc(k.sems["silu_used"], 1)
                at = bass.ds(p, 1) if not isinstance(p, int) else slice(p, p + 1)
                chain.link(dve.tensor_copy(k.act_hi[:, at, :T], k.f_t[:, :T].unsqueeze(1)))
                chain.link(dve.tensor_tensor(k.act_lo[:, at, :T], k.f_t[:, :T].unsqueeze(1), k.act_hi[:, at, :T].bitcast(F32), ALU.subtract))
            return

        def empty(scale):
            def body(m, i, e):
                s = self.slot(e)
                dve.wait_ge(k.sems["slab_mm"], m + (self.b_mm + 1))
                at = bass.ds(m, 1) if not isinstance(m, int) else slice(m, m + 1)
                dst, src = self.dst[:, at, :T], flat(k.ps[:, 2 * s:2 * s + 2])[:, :T].unsqueeze(1)
                if self.mode == "add":
                    ins = dve.tensor_tensor(dst, src, dst, ALU.add)
                elif scale != 1.0:
                    ins = dve.tensor_scalar(dst, src, scale, None, ALU.mult)
                else:
                    ins = dve.tensor_copy(dst, src)
                ins.then_inc(k.sems[f"psum_free{s}"], 1)
            return body

        for m0, m1, scale in self.segs:
            self.slabs(dve, empty(scale), m0, m1)


class Rope(Stage):

    def __init__(self, kit, t, m0, m1, rot, table, hi=None, lo=None, lo0=0, T=SEQ):
        super().__init__(kit)
        self.t, self.m0, self.n, self.rot, self.table = t, m0, m1 - m0, rot, table
        self.hi, self.lo, self.lo0, self.T = hi, lo, lo0, T
        self.b_mm = kit.reserve("rot_mm", self.n)
        self.b_c = kit.reserve("rot_cos", self.n)
        self.b_a = kit.reserve("rot_sum", self.n)
        self.b_h = kit.reserve("rot_hi", self.n if lo is not None else 0)
        self.b_d = kit.reserve("rot_done", self.n if lo is not None else 0)

    def turns(self, eng, body, chain=None, per=0):
        if self.n >= 6 and self.n % 2 == 0:
            with (chain.loop(self.n // 2, 2 * per) if chain else eng.Fori(0, self.n // 2)) as i:
                for e in range(2):
                    body(i * 2 + e, e)
        else:
            for m in range(self.n):
                body(m, m)

    def at(self, m, first=None):
        first = self.m0 if first is None else first
        return bass.ds(m + first, 1) if not isinstance(m, int) else slice(first + m, first + m + 1)

    def before(self, eng, name, base, m, lag):
        if not isinstance(m, int) or m >= lag:
            eng.wait_ge(self.kit.sems[name], m + (base + 1 - lag))

    def tensor(self, pe):
        k = self.kit

        def body(m, e):
            self.before(pe, "rot_sum", self.b_a, m, 2)
            pe.matmul(k.ps[:, e % 2, :], self.rot, self.t[:, self.at(m), 0:SEQ], start=True, stop=True).then_inc(k.sems["rot_mm"], 1)
        self.turns(pe, body)

    def gpsimd(self, pool, chain):
        k = self.kit

        def body(m, e):
            self.before(pool, "rot_sum", self.b_a, m, 2)
            pool.tensor_tensor(k.rot_c[:, e % 2, :].unsqueeze(1), self.t[:, self.at(m), 0:SEQ], self.table[:, 0, :].unsqueeze(1), ALU.mult).then_inc(k.sems["rot_cos"], 1)
        self.turns(pool, body)

    def scalar(self, act, chain):
        k, T = self.kit, self.T
        if self.lo is None:
            return

        def body(m, e):
            if T > SEQ:
                self.before(act, "rot_done", self.b_d, m, 2)
                chain.link(act.activation(k.rot_q[:, e % 2, SEQ:T].unsqueeze(1), self.t[:, self.at(m), SEQ:T], ACT.Copy))
            act.wait_ge(k.sems["rot_sum"], m + (self.b_a + 1))
            act.activation(self.hi[:, self.at(m), 0:T], k.rot_q[:, e % 2, 0:T].unsqueeze(1), ACT.Copy).then_inc(k.sems["rot_hi"], 1)
        self.turns(act, body, chain if T > SEQ else None, 1)

    def vector(self, dve, chain):
        k, T = self.kit, self.T

        def low(m, e):
            dve.wait_ge(k.sems["rot_hi"], m + (self.b_h + 1))
            dve.tensor_tensor(self.lo[:, self.at(m, self.lo0), 0:T], k.rot_q[:, e % 2, 0:T].unsqueeze(1), self.hi[:, self.at(m), 0:T].bitcast(F32),
                              ALU.subtract).then_inc(k.sems["rot_done"], 1)

        def body(m, e):
            dve.wait_ge(k.sems["rot_mm"], m + (self.b_mm + 1))
            self.before(dve, "rot_sum", self.b_a, m, 1)
            chain.link(dve.tensor_tensor(k.rot_s[:], k.ps[:, e % 2, :], self.table[:, 1, :], ALU.mult))
            dve.wait_ge(k.sems["rot_cos"], m + (self.b_c + 1))
            if self.lo is None:
                dve.tensor_tensor(self.t[:, self.at(m), 0:SEQ], k.rot_s[:].unsqueeze(1), k.rot_c[:, e % 2, :].unsqueeze(1), ALU.add).then_inc(k.sems["rot_sum"], 1)
            else:
                self.before(dve, "rot_done", self.b_d, m, 2)
                dve.tensor_tensor(k.rot_q[:, e % 2, 0:SEQ], k.rot_s[:], k.rot_c[:, e % 2, :], ALU.add).then_inc(k.sems["rot_sum"], 1)
                low(m, e)
        self.turns(dve, body, chain, 1)


class Transposes(Stage):

    def __init__(self, kit, batches):
        super().__init__(kit)
        self.batches = batches
        self.b_t = kit.reserve("tp_ready", len(batches))
        self.b_f = kit.reserve("tp_free", len(batches))
        self.b_h = kit.reserve("tp_hi", sum(1 for b in batches if b[3]))

    def bank(self, n):
        return 2 + n % 4

    def tensor(self, pe):
        k = self.kit
        for n, (blocks, parts, _, _) in enumerate(self.batches):
            if n >= 4:
                pe.wait_ge(k.sems["tp_free"], self.b_f + n - 3)
            for src, col in blocks:
                rows, cols = src.shape[0], src.shape[1]
                ins = pe.transpose(k.ps[0:cols, self.bank(n), col:col + rows], src, k.ident[0:rows, 0:rows])
            ins.then_inc(k.sems["tp_ready"], 1)

    def scalar(self, act, chain):
        k, h = self.kit, 0
        for n, (_, parts, _, high) in enumerate(self.batches):
            if high:
                act.wait_ge(k.sems["tp_ready"], self.b_t + n + 1)
                high(act, k.ps[0:parts, self.bank(n), :]).then_inc(k.sems["tp_hi"], 1)

    def vector(self, dve, chain):
        k, h = self.kit, 0
        for n, (_, parts, out, high) in enumerate(self.batches):
            if high:
                h += 1
                dve.wait_ge(k.sems["tp_hi"], self.b_h + h)
            else:
                dve.wait_ge(k.sems["tp_ready"], self.b_t + n + 1)
            out(dve, k.ps[0:parts, self.bank(n), :]).then_inc(k.sems["tp_free"], 1)


class Attend(Stage):

    def __init__(self, kit, J, batches, preload, stage, scores, tiles, slots, pv, prepare, marks, finish, pt, spread=False, sink=None, v_stage=None):
        super().__init__(kit)
        self.pt, self.v_stage = pt, v_stage
        self.J, self.batches, self.preload, self.stage, self.scores = J, batches, preload, stage, scores
        self.tiles, self.slots, self.pv, self.prepare, self.marks, self.finish = tiles, slots, pv, prepare, marks, finish
        self.spread, self.sink = spread, sink
        self.units = [(a, qi, n, i, tr) for n, batch in enumerate(batches) for a, qi, i, tr in batch]
        self.U, self.B = len(self.units), len(batches)
        assert self.U % 2 == 0 and self.B % 2 == 0
        self.ca = [int(tr) for *_, tr in self.units]
        self.cb = [int(tr and len(tiles(qi)) > 1) for _, qi, _, _, tr in self.units]
        self.copies = [len(stage(0, n)) for n in range(self.B)]
        n = J * self.U
        self.b = {s: kit.reserve(s, c) for s, c in (
            ("scores_ready", n), ("neg_max", n), ("probs_ready", n), ("prepared", n), ("tr_a", J * sum(self.ca)), ("tr_b", J * sum(self.cb)),
            ("pt_a", J * sum(self.ca)), ("pt_b", J * sum(self.cb)), ("pv_ready", J * self.B), ("o_free", J * self.B),
            ("spread_ready", J * self.B * int(spread)))}
        self.b_keys = kit.dma_count("keys_in", len(preload))
        self.b_v = kit.dma_count("v_staged", J * int(v_stage is not None))
        self.b_stage = [kit.dma_count(f"q_staged{p}", J * sum(self.copies[p::2])) for p in range(2)]

    def turns(self, eng, body, chain=None, per=0):
        if self.J > 2:
            if chain is None:
                with eng.Fori(0, self.J - 1) as j:
                    body(j, False)
            else:
                with chain.loop(self.J - 1, per) as j:
                    body(j, False)
        else:
            for j in range(self.J - 1):
                body(j, False)
        body(self.J - 1, True)

    def g(self, j, u, name, plus=0):
        return j * self.U + (u + self.b[name] + plus)

    def gt(self, j, u, name, plus=0):
        c = self.ca if name.endswith("a") else self.cb
        return j * sum(c) + (sum(c[:u]) + self.b[name] + plus)

    def gb(self, j, n, name, plus=0):
        return j * self.B + (n + self.b[name] + plus)

    def sc(self, u, n):
        s = u % 2
        return flat(self.kit.ps[:, 2 * s:2 * s + 2])[:, :n]

    def finished(self, u):
        ends = lambda v: v >= 0 and (v + 1 == self.U or self.units[v + 1][2] != self.units[v][2])
        return [self.units[v][2] for v in (u - 1, u) if ends(v) and (v == u - 1 or v + 1 == self.U)]

    def ahead(self, j, last, u, by, body):
        if u + by < self.U:
            body(j, u + by)
        elif not last:
            body(j + 1, u + by - self.U)

    def sync(self, sp):
        k = self.kit
        self.enter(sp)
        for dst, src in self.preload:
            sp.dma_start(dst.bitcast(F32), src.bitcast(F32)).then_inc(k.sems["keys_in"], 16)

        def move(j, n):
            for dst, src in self.stage(j, n):
                sp.dma_start(dst.bitcast(F32), src.bitcast(F32)).then_inc(k.sems[f"q_staged{n % 2}"], 16)

        for n in range(self.B):
            move(0, n)
        if self.v_stage:
            sp.dma_start(*self.v_stage(0)).then_inc(k.sems["v_staged"], 16)

        def turn(j, last):
            u = 0
            if self.v_stage:
                if not last:
                    sp.wait_ge(k.sems["scores_ready"], self.g(j, self.U, "scores_ready"))
                    for n in range(self.B):
                        move(j + 1, n)
                    sp.wait_ge(k.sems["pv_ready"], self.gb(j, self.B, "pv_ready"))
                    sp.dma_start(*self.v_stage(j + 1)).then_inc(k.sems["v_staged"], 16)
                return
            for n, batch in enumerate(self.batches):
                u += len(batch)
                if not last:
                    sp.wait_ge(k.sems["scores_ready"], self.g(j, u, "scores_ready"))
                    move(j + 1, n)
        self.turns(sp, turn)

    def tensor(self, pe):
        k, S = self.kit, self.kit.sems

        def qk(j, u):
            a, qi, n, i, tr = self.units[u]
            if sum(self.copies) and (u == 0 or self.units[u - 1][2] != n):
                p = n % 2
                pe.wait_ge(S[f"q_staged{p}"], j * (16 * sum(self.copies[p::2])) + (self.b_stage[p] + 16 * sum(self.copies[p:n + 1:2])))
            self.scores(pe, self.sc(u, 1024), j, a, qi).then_inc(S["scores_ready"], 1)

        def turn_round(j, u):
            a, qi, n, i, tr = self.units[u]
            nt = len(self.tiles(qi))
            na = (nt + 1) // 2
            pe.wait_ge(S["prepared"], self.g(j, u, "prepared", 1))
            if tr:
                pe.wait_ge(S["pt_a"], self.gt(j, u, "pt_a"))
                for t in range(na):
                    ins = pe.transpose(k.ps[:, 4, t * P:(t + 1) * P], k.probs[:, u % 2, t * P:(t + 1) * P], k.ident[:])
                ins.then_inc(S["tr_a"], 1)
                if nt > na:
                    pe.wait_ge(S["pt_b"], self.gt(j, u, "pt_b"))
                    for t in range(na, nt):
                        ins = pe.transpose(k.ps[:, 5, (t - na) * P:(t - na + 1) * P], k.probs[:, u % 2, t * P:(t + 1) * P], k.ident[:])
                    ins.then_inc(S["tr_b"], 1)

        def output(j, n):
            end = max(u for u in range(self.U) if self.units[u][2] == n)
            pe.wait_ge(S["pt_a"], self.gt(j, end + 1, "pt_a"))
            pe.wait_ge(S["pt_b"], self.gt(j, end + 1, "pt_b"))
            pe.wait_ge(S["o_free"], self.gb(j, n, "o_free", -1))
            if self.v_stage and n == 0:
                pe.wait_ge(S["v_staged"], j * 16 + (self.b_v + 16))
            self.pv(pe, k.ps[:, 6 + n % 2, :], j, n).then_inc(S["pv_ready"], 1)

        def turn(j, last):
            for u in range(self.U):
                if u + 1 == self.U:
                    turn_round(j, u)
                pe.wait_ge(S["probs_ready"], self.g(j, u, "probs_ready", 1))
                self.ahead(j, last, u, 2, qk)
                if u + 1 < self.U:
                    turn_round(j, u)
                for n in self.finished(u):
                    output(j, n)

        if self.preload:
            pe.wait_ge(S["keys_in"], self.b_keys + 16 * len(self.preload))
        qk(0, 0)
        qk(0, 1)
        self.turns(pe, turn)

    def vector(self, dve, chain):
        k, S = self.kit, self.kit.sems

        def neg_max(j, u):
            a, qi, *_ = self.units[u]
            n = len(self.tiles(qi)) * P
            dve.wait_ge(S["scores_ready"], self.g(j, u, "scores_ready", 1))
            ins = dve.tensor_reduce(k.nm[:, u % 2, 0:1], self.sc(u, n), AX.X, ALU.max, negate=True)
            if self.sink:
                chain.link(ins)
                ins = dve.tensor_tensor(k.nm[:, u % 2, 0:1], k.nm[:, u % 2, 0:1], self.sink(j, a)[0], ALU.min)
            ins.then_inc(S["neg_max"], 1)

        def prepare(j, u):
            a, qi, *_ = self.units[u]
            dve.wait_ge(S["probs_ready"], self.g(j, u, "probs_ready", 1))
            den = k.rowsum[:, u % 2, 0:1]
            if self.sink:
                chain.link(dve.tensor_tensor(k.den[:, u % 2, 0:1], den, k.sink_exp[:, u % 2, 0:1], ALU.add))
                den = k.den[:, u % 2, 0:1]
            chain_ins = dve.reciprocal(k.rinv[:, u:u + 1], den)
            if self.prepare is not None:
                chain.link(chain_ins)
                dve.wait_ge(S["prepared"], self.g(j, u, "prepared"))
                chain_ins = self.prepare(dve, chain, j, u, a, qi, k.probs[:, u % 2, 0:len(self.tiles(qi)) * P], k.rinv[:, u:u + 1])
            chain_ins.then_inc(S["prepared"], 1)

        def turn(j, last):
            for u, (a, qi, n, i, tr) in enumerate(self.units):
                nt = len(self.tiles(qi))
                na = (nt + 1) // 2
                if u + 1 < self.U:
                    self.ahead(j, last, u, 2, neg_max)
                    self.ahead(j, last, u, 1, prepare)
                if tr:
                    s0 = self.slots(n, qi)
                    dve.wait_ge(S["tr_a"], self.gt(j, u, "tr_a", 1))
                    dve.tensor_copy(self.turned(n, a, s0, s0 + na, i), k.ps[:, 4, 0:na * P].rearrange("p (t c) -> p t c", c=P)).then_inc(S["pt_a"], 1)
                if u + 1 == self.U:
                    self.ahead(j, last, u, 1, prepare)
                    self.ahead(j, last, u, 2, neg_max)
                for m in self.finished(u):
                    if self.spread:
                        dve.wait_ge(S["spread_ready"], self.gb(j, m, "spread_ready", 1))
                    else:
                        dve.wait_ge(S["pv_ready"], self.gb(j, m, "pv_ready", 1))
                    self.finish(dve, chain, k.ps[:, 6 + m % 2, :], j, m).then_inc(S["o_free"], 1)

        neg_max(0, 0)
        neg_max(0, 1)
        prepare(0, 0)
        pm, fm = self.marks
        per = self.U * ((2 if self.sink else 0)) + sum((1 + pm(u)) if self.prepare is not None else 0 for u in range(self.U)) + fm * self.B
        self.turns(dve, turn, chain, per)

    def turned(self, n, a, s0, s1, i):
        return self.pt[:, n % 2, a % 2, s0:s1, i * P:(i + 1) * P]

    def scalar(self, act, chain):
        k, S = self.kit, self.kit.sems

        def exp(j, u):
            a, qi, *_ = self.units[u]
            n = len(self.tiles(qi)) * P
            act.wait_ge(S["neg_max"], self.g(j, u, "neg_max", 1))
            ins = act.activation(k.probs[:, u % 2, 0:n], self.sc(u, n), ACT.Exp, bias=k.nm[:, u % 2, 0:1],
                                 accum_out=k.rowsum[:, u % 2, 0:1])
            if self.sink:
                ins = act.activation(k.sink_exp[:, u % 2, 0:1], self.sink(j, a)[1], ACT.Exp, bias=k.nm[:, u % 2, 0:1])
            ins.then_inc(S["probs_ready"], 1)

        def turn(j, last):
            for u, (a, qi, n, i, tr) in enumerate(self.units):
                nt = len(self.tiles(qi))
                na = (nt + 1) // 2
                if tr and nt > na:
                    s0 = self.slots(n, qi)
                    act.wait_ge(S["tr_b"], self.gt(j, u, "tr_b", 1))
                    act.activation(self.turned(n, a, s0 + na, s0 + nt, i), k.ps[:, 5, 0:(nt - na) * P].rearrange("p (t c) -> p t c", c=P), ACT.Copy).then_inc(S["pt_b"], 1)
                if tr and nt == na:
                    act.wait_ge(S["tr_a"], self.gt(j, u, "tr_a", 1))
                if not tr:
                    act.wait_ge(S["prepared"], self.g(j, u, "prepared", 2))
                self.ahead(j, last, u, 2, exp)
                for m in self.finished(u) if self.spread else []:
                    act.wait_ge(S["pv_ready"], self.gb(j, m, "pv_ready", 1))
                    act.wait_ge(S["o_free"], self.gb(j, m, "o_free"))
                    act.activation(k.spread[:], k.ps[:, 6 + m % 2, 256:512], ACT.Copy).then_inc(S["spread_ready"], 1)

        exp(0, 0)
        exp(0, 1)
        self.turns(act, turn)


class Load(Stage):

    def __init__(self, kit, loads):
        super().__init__(kit)
        self.loads = loads
        self.b = kit.side_in
        kit.side_in += 16 * len(loads)
        kit.sem("side_in")

    def scalar(self, act, chain):
        for dst, src in self.loads:
            act.dma_start(dst, src).then_inc(self.kit.sems["side_in"], 16)
        act.wait_ge(self.kit.sems["side_in"], self.b + 16 * len(self.loads))


class Scale(Stage):

    def __init__(self, kit, steps):
        super().__init__(kit)
        self.steps = steps

    def vector(self, dve, chain):
        self.steps(dve, chain)


class HeadNorm(Stage):

    def __init__(self, kit, tiles, n, block, T):
        super().__init__(kit)
        self.tiles, self.n, self.block, self.T = tiles, n, block, T
        c = len(tiles)
        self.b = {s: kit.reserve(s, c) for s in ("hn_sq", "hn_sum", "hn_std", "hn_done")}

    def scalar(self, act, chain):
        k, S, T = self.kit, self.kit.sems, self.T
        for i in range(len(self.tiles) + 1):
            if i < len(self.tiles):
                act.activation(k.hn_sq[:, i % 2, :T], self.tiles[i][0], ACT.Square).then_inc(S["hn_sq"], 1)
            if i >= 1:
                act.wait_ge(S["hn_sum"], self.b["hn_sum"] + i)
                if i >= 3:
                    act.wait_ge(S["hn_done"], self.b["hn_done"] + i - 2)
                act.activation(k.hn_std[:, (i - 1) % 2, :T], flat(k.ps[:, 2 * ((i - 1) % 2):2 * ((i - 1) % 2) + 2])[:, :T], ACT.Sqrt,
                               bias=k.eps[:, 0:1], scale=1.0 / self.n).then_inc(S["hn_std"], 1)

    def tensor(self, pe):
        k, S, T = self.kit, self.kit.sems, self.T
        for i in range(len(self.tiles)):
            pe.wait_ge(S["hn_sq"], self.b["hn_sq"] + i + 1)
            if i >= 2:
                pe.wait_ge(S["hn_std"], self.b["hn_std"] + i - 1)
            for t0 in range(0, T, 512):
                t1 = min(T, t0 + 512)
                ins = pe.matmul(k.ps[:, 2 * (i % 2) + t0 // 512, 0:t1 - t0], self.block, k.hn_sq[:, i % 2, t0:t1], start=True, stop=True)
            ins.then_inc(S["hn_sum"], 1)

    def vector(self, dve, chain):
        k, S, T = self.kit, self.kit.sems, self.T
        for i, (t, gain) in enumerate(self.tiles):
            dve.wait_ge(S["hn_std"], self.b["hn_std"] + i + 1)
            if i >= 1:
                dve.wait_ge(S["hn_done"], self.b["hn_done"] + i)
            chain.link(dve.reciprocal(k.hn_r[:, :T], k.hn_std[:, i % 2, :T]))
            dve.scalar_tensor_tensor(t, t, gain, k.hn_r[:, :T], ALU.mult, ALU.mult).then_inc(S["hn_done"], 1)


class Products(Stage):

    def __init__(self, kit, jobs):
        super().__init__(kit)
        self.jobs = jobs
        self.b_m = kit.reserve("job_mm", len(jobs))
        self.b_f = kit.reserve("job_free", len(jobs))
        self.b_h = kit.reserve("job_hi", sum(1 for j in jobs if j[2]))

    def tensor(self, pe):
        k, S = self.kit, self.kit.sems
        for n, (mms, out, high) in enumerate(self.jobs):
            if n >= 2:
                pe.wait_ge(S["job_free"], self.b_f + n - 1)
            for ins in mms(pe, k.ps[:, 2 * (n % 2):2 * (n % 2) + 2]):
                last = ins
            last.then_inc(S["job_mm"], 1)

    def scalar(self, act, chain):
        k, S = self.kit, self.kit.sems
        for n, (_, out, high) in enumerate(self.jobs):
            if high:
                act.wait_ge(S["job_mm"], self.b_m + n + 1)
                high(act, k.ps[:, 2 * (n % 2):2 * (n % 2) + 2]).then_inc(S["job_hi"], 1)

    def vector(self, dve, chain):
        k, S, h = self.kit, self.kit.sems, 0
        for n, (_, out, high) in enumerate(self.jobs):
            dve.wait_ge(S["job_mm"], self.b_m + n + 1)
            if high:
                h += 1
                dve.wait_ge(S["job_hi"], self.b_h + h)
            out(dve, chain, k.ps[:, 2 * (n % 2):2 * (n % 2) + 2]).then_inc(S["job_free"], 1)


class WindowMeans(Stage):

    def __init__(self, kit, u0):
        super().__init__(kit)
        self.u0 = u0
        self.spans = [(0, SEQ), (SEQ, TOK)]

    def vector(self, dve, chain):
        k = self.kit
        for b in range(3):
            ins = dve.memset(k.pad[:, b, :], 0.0)
        chain.link(ins)
        for g, w in enumerate(WINDOWS):
            for t0, t1 in self.spans:
                n = t1 - t0
                u = k.qkv[:, self.u0 + g, t0:t1]
                chain.link(dve.memset(k.pad[:, 0, 8 + n:24 + n], 0.0))
                chain.link(dve.tensor_copy(k.pad[:, 0, 8:8 + n], u))
                src, step, at = 0, 1, 0
                while step < w:
                    dst = 1 + at % 2
                    width = 8 + n + 16 - step
                    chain.link(dve.tensor_tensor(k.pad[:, dst, 0:width - step], k.pad[:, src, 0:width - step], k.pad[:, src, step:width], ALU.add))
                    src, step, at = dst, step * 2, at + 1
                lo = 8 - w // 2
                chain.link(dve.tensor_tensor(k.mean[:, g, t0:t1], k.pad[:, src, lo:lo + n], k.inv_cnt[:, g, t0:t1], ALU.mult))
                chain.link(dve.tensor_tensor(k.mean[:, g, t0:t1], k.mean[:, g, t0:t1], u, ALU.subtract))


class Indexer(Stage):

    def __init__(self, kit, iq0, ik):
        super().__init__(kit)
        self.iq0, self.ik = iq0, ik
        self.J, self.U = 4, 8
        n = self.J * self.U
        self.b = {s: kit.reserve(s, c) for s, c in (("iq_staged", self.J * 2), ("scores_ready", n), ("idx_relu", n), ("idx_acc", n))}

    def gpsimd(self, pool, chain):
        k, b = self.kit, self.b

        def copy(j, a):
            at = bass.ds(j + self.iq0, 1) if not isinstance(j, int) else slice(self.iq0 + j, self.iq0 + j + 1)
            rows = slice(64 * a, 64 * a + 64)
            pool.tensor_copy(k.iq_s[rows, :].unsqueeze(1), k.qkv2[rows, at, :]).then_inc(k.sems["iq_staged"], 1)

        copy(0, 0)
        copy(0, 1)
        with pool.Fori(0, self.J - 1) as j:
            for a in range(2):
                pool.wait_ge(k.sems["scores_ready"], j * self.U + (b["scores_ready"] + 4 * a + 4))
                copy(j + 1, a)

    def tensor(self, pe):
        k, b = self.kit, self.b
        with pe.Fori(0, self.J) as j:
            for u in range(self.U):
                a, qi = u // 4, u % 4
                rows, n = slice(64 * a, 64 * a + 64), (qi + 1) * P
                if qi == 0:
                    pe.wait_ge(k.sems["iq_staged"], j * 2 + (b["iq_staged"] + a + 1))
                pe.wait_ge(k.sems["idx_relu"], j * self.U + (b["idx_relu"] + u - 3))
                pe.matmul(k.ps[:, u % 4, 0:n], k.iq_s[rows, qi * P:(qi + 1) * P], self.ik[rows, 0:n], start=True, stop=True).then_inc(k.sems["scores_ready"], 1)

    def scalar(self, act, chain):
        k, b = self.kit, self.b
        with act.Fori(0, self.J) as j:
            for u in range(self.U):
                n = (u % 4 + 1) * P
                act.wait_ge(k.sems["scores_ready"], j * self.U + (b["scores_ready"] + u + 1))
                act.wait_ge(k.sems["idx_acc"], j * self.U + (b["idx_acc"] + u - 1))
                act.activation(k.rel[:, u % 2, 0:n], k.ps[:, u % 4, 0:n], ACT.Relu).then_inc(k.sems["idx_relu"], 1)

    def vector(self, dve, chain):
        k, b = self.kit, self.b
        chain.link(dve.memset(k.iscore[:], 0.0))
        with dve.Fori(0, self.J) as j:
            for u in range(self.U):
                a, qi = u // 4, u % 4
                n = (qi + 1) * P
                dve.wait_ge(k.sems["idx_relu"], j * self.U + (b["idx_relu"] + u + 1))
                dve.wait_ge(k.sems["idx_acc"], j * self.U + (b["idx_acc"] + u - 2))
                at = bass.ds(j * 2 + a, 1)
                dve.scalar_tensor_tensor(k.iscore[:, qi, 0:n], k.rel[:, u % 2, 0:n], k.iw[:, qi, at], k.iscore[:, qi, 0:n], ALU.mult, ALU.add).then_inc(k.sems["idx_acc"], 1)


class TopK(Stage):

    def __init__(self, kit):
        super().__init__(kit)
        kit.reserve("rounds", 2 * (TOPK // 8))

    def vector(self, dve, chain):
        k = self.kit
        for qi in range(1, QT):
            d = slice(qi * P, (qi + 1) * P)
            ins = dve.tensor_tensor(k.iscore[:, qi, d], k.iscore[:, qi, d], k.causal, ALU.add)
        chain.link(ins)
        dve.tensor_copy(k.chosen[:, 0, 0:P], k.causal)
        with chain.loop(TOPK // 8, 2) as i:
            for qi in range(1, QT):
                ins = dve.max(k.top8[:, qi, :], k.iscore[:, qi, 0:(qi + 1) * P])
            chain.link(ins)
            dve.sem_inc(k.sems["rounds"], 1)
            for qi in range(1, QT):
                s = k.iscore[:, qi, 0:(qi + 1) * P]
                ins = dve.match_replace(s, k.top8[:, qi, :], s, TAKEN)
            chain.link(ins)
            dve.sem_inc(k.sems["rounds"], 1)
        for qi in range(1, QT):
            n = (qi + 1) * P
            dve.tensor_scalar(k.chosen[:, qi, 0:n], k.iscore[:, qi, 0:n], -2e38, NEG, ALU.is_gt, ALU.mult)


class CmpAttend(Stage):

    def __init__(self, kit, q0):
        super().__init__(kit)
        self.q0 = q0
        self.b = {s: kit.reserve(s, 8) for s in ("cs_mm", "cs_sub", "cs_exp", "cs_p", "cs_tr", "cs_pa", "cs_pb", "cs_pv", "cs_out")}

    def head(self, n, a):
        return 8 * (n // 4) + 4 * a + n % 4

    def tensor(self, pe):
        k, b, S = self.kit, self.b, self.kit.sems

        def qk(n):
            if n >= 2:
                pe.wait_ge(S["cs_sub"], b["cs_sub"] + n - 1)
            for a in range(2):
                rows = slice(64 * a, 64 * a + 64)
                for qi in range(QT):
                    c, bank = qi * 32, 2 * (n % 2) + a
                    pe.matmul(k.ps[:, bank, c:c + 32], k.qkv2[rows, self.q0 + n, qi * P:(qi + 1) * P], k.k_cmp[rows, n // 4, :],
                              start=True, stop=False, skip_group_check=True)
                    ins = pe.matmul(k.ps[:, bank, c:c + 32], k.ident_b, k.cmp_mask[:, qi, :], start=False, stop=True, skip_group_check=True)
            ins.then_inc(S["cs_mm"], 1)

        qk(0)
        for n in range(8):
            if n + 1 < 8:
                qk(n + 1)
            pe.wait_ge(S["cs_p"], b["cs_p"] + n + 1)
            if n >= 1:
                pe.wait_ge(S["cs_pa"], b["cs_pa"] + n)
                pe.wait_ge(S["cs_pb"], b["cs_pb"] + n)
            for a in range(2):
                for qi in range(QT):
                    c = (a * QT + qi) * 32
                    ins = pe.transpose(k.ps[0:32, 4 + a, qi * P:(qi + 1) * P], k.c_p[:, c:c + 32], k.ident[:])
            ins.then_inc(S["cs_tr"], 1)
            pe.wait_ge(S["cs_pa"], b["cs_pa"] + n + 1)
            pe.wait_ge(S["cs_pb"], b["cs_pb"] + n + 1)
            if n >= 2:
                pe.wait_ge(S["cs_out"], b["cs_out"] + n - 1)
            for a in range(2):
                kv = 2 * (n // 4) + a
                ins = pe.matmul(k.ps[64 * a:64 * a + 64, 6 + n % 2, :], k.v_cmp[0:32, kv * HD:(kv + 1) * HD], k.c_pt[0:32, a, :], start=True, stop=True)
            ins.then_inc(S["cs_pv"], 1)

    def vector(self, dve, chain):
        k, b, S = self.kit, self.b, self.kit.sems
        bc = lambda ap: ap.unsqueeze(2).to_broadcast([P, 8, 32])
        v3 = lambda ap: ap.rearrange("p (u n) -> p u n", n=32)
        for n in range(8):
            dve.wait_ge(S["cs_mm"], b["cs_mm"] + n + 1)
            s = k.ps[:, 2 * (n % 2):2 * (n % 2) + 2, 0:P].rearrange("p a (q n) -> p a q n", n=32)
            m = k.c_m[:, 0:8].rearrange("p (a q) -> p a q", q=QT)
            chain.link(dve.tensor_reduce(m, s, AX.X, ALU.max, negate=True))
            dve.tensor_tensor(k.c_s[:].rearrange("p (a q n) -> p a q n", q=QT, n=32), s, m.unsqueeze(3).to_broadcast([P, 2, QT, 32]), ALU.add).then_inc(S["cs_sub"], 1)
            dve.wait_ge(S["cs_exp"], b["cs_exp"] + n + 1)
            chain.link(dve.tensor_reduce(k.c_r[:, 0:8], v3(k.c_e[:]), AX.X, ALU.add))
            chain.link(dve.reciprocal(k.c_r[:, 8:16], k.c_r[:, 0:8]))
            for a in range(2):
                ins = dve.tensor_tensor(k.c_r[:, 16 + 4 * a:20 + 4 * a], k.c_r[:, 8 + 4 * a:12 + 4 * a], k.gate_cmp[:, :, self.head(n, a) * 3], ALU.mult)
            chain.link(ins)
            dve.tensor_tensor(v3(k.c_p[:]), v3(k.c_e[:]), bc(k.c_r[:, 16:24]), ALU.mult).then_inc(S["cs_p"], 1)
            dve.wait_ge(S["cs_tr"], b["cs_tr"] + n + 1)
            dve.tensor_copy(k.c_pt[0:32, 0, :], k.ps[0:32, 4, :]).then_inc(S["cs_pa"], 1)
            dve.wait_ge(S["cs_pv"], b["cs_pv"] + n + 1)
            dve.tensor_copy(k.o_t[:, n, :], k.ps[:, 6 + n % 2, :]).then_inc(S["cs_out"], 1)

    def scalar(self, act, chain):
        k, b, S = self.kit, self.b, self.kit.sems
        for n in range(8):
            act.wait_ge(S["cs_sub"], b["cs_sub"] + n + 1)
            act.activation(k.c_e[:], k.c_s[:], ACT.Exp).then_inc(S["cs_exp"], 1)
            act.wait_ge(S["cs_tr"], b["cs_tr"] + n + 1)
            act.activation(k.c_pt[0:32, 1, :], k.ps[0:32, 5, :], ACT.Copy).then_inc(S["cs_pb"], 1)


class Doubled(Stage):

    def __init__(self, kit, src):
        super().__init__(kit)
        self.src = src
        self.b = kit.dma_count("doubled", 4)

    def gpsimd(self, pool, chain):
        pass

    def scalar(self, act, chain):
        k = self.kit
        for e in range(2):
            rows = slice(64 * e, 64 * e + 64)
            act.dma_start(k.kc2[0:64, e:4:2, :], k.qkv2[rows, self.src:self.src + 2, :]).then_inc(k.sems["doubled"], 16)
            act.dma_start(k.kc2[64:128, e:4:2, 0:SEQ - 1], k.qkv2[rows, self.src:self.src + 2, 1:SEQ]).then_inc(k.sems["doubled"], 16)
        act.wait_ge(k.sems["doubled"], self.b + 64)


class Split(Stage):

    def __init__(self, kit, tiles, in_place=False):
        super().__init__(kit)
        self.tiles, self.in_place = tiles, in_place
        self.b = kit.reserve("split_hi", len(tiles))
        self.b_lo = kit.reserve("split_lo", len(tiles))

    def scalar(self, act, chain):
        k, S = self.kit, self.kit.sems
        for n, (src, hi, lo) in enumerate(self.tiles):
            if n >= 2:
                act.wait_ge(S["split_lo"], self.b_lo + n - 1)
            if self.in_place:
                chain.link(act.activation(k.split_t[:, n % 2, :], src, ACT.Copy))
                src = k.split_t[:, n % 2, :]
            act.activation(hi, src, ACT.Copy).then_inc(S["split_hi"], 1)

    def vector(self, dve, chain):
        k, S = self.kit, self.kit.sems
        for n, (src, hi, lo) in enumerate(self.tiles):
            dve.wait_ge(S["split_hi"], self.b + n + 1)
            dve.tensor_tensor(lo, k.split_t[:, n % 2, :] if self.in_place else src, hi.bitcast(F32), ALU.subtract).then_inc(S["split_lo"], 1)


class Store(Stage):

    def __init__(self, kit, out, src):
        super().__init__(kit)
        self.out, self.src = out, src
        kit.sem("stored")

    def scalar(self, act, chain):
        act.dma_start(self.out, self.src).then_inc(self.kit.sems["stored"], 16)
        act.wait_ge(self.kit.sems["stored"], 16)


class Step(Stage):

    def __init__(self, kit, act_part):
        super().__init__(kit)
        self.act_part = act_part

    def scalar(self, act, chain):
        self.act_part(act, chain)


def memory(kit):
    H, A, Y, TMP, W, C = 24576, 73728, 122880, 147456, 159744, 184320
    k, at = kit, kit.at
    k.x = at("x", [P, DC, TOK], F32, 0)
    k.h_hi = at("h_hi", [P, DC, TOK], F32R, H)
    k.h_lo = at("h_lo", [P, DC, TOK], F32R, H + 24576)
    k.act_hi = at("act_hi", [P, KMAX, TOK], F32R, A)
    k.act_lo = at("act_lo", [P, KMAX, TOK], F32R, A + 24576)
    k.y = at("y", [P, DC, TOK], F32, Y)
    k.f_s = at("f_s", [P, TOK], F32, TMP)
    k.f_t = at("f_t", [P, TOK], F32, TMP + 3072)
    k.w_raw = at("w_raw", [P, 2, KMAX * P], F32, W)
    k.w_hi = at("w_hi", [P, 2, KMAX * P], F32R, W + 8192)
    k.w_lo = at("w_lo", [P, 2, KMAX * P], F32R, W + 16384)
    k.final = at("final", [P, DC, SEQ], F32, Y)
    k.mod_ring = at("mod_ring", [P, Modulation.TURN_PE, 2 * DC * P], F32, H)
    k.c_all = at("c_all", [P, 2, D], F32, H + 40960)
    k.row_ring = at("row_ring", [P, Modulation.TURN_BOTH + Modulation.TURN_X, 2 * D], F32, A)
    k.row_out = at("row_out", [P, 4, D], F32, A + 57344)
    k.n_sq = at("n_sq", [P, 2, TOK], F32, A)
    k.n_t = at("n_t", [P, 2, TOK], F32, A + 6144)
    k.n_h = at("n_h", [P, 2, TOK], F32, A + 12288)
    k.n_rs = at("n_rs", [P, TOK], F32, A + 18432)
    k.n_r = at("n_r", [P, TOK], F32, A + 21504)
    k.qkv, k.qkv_hi = at("qkv", [P, 12, TOK], F32, A), at("qkv_hi", [P, 12, TOK], F32R, A)
    k.qkv2, k.qkv2_hi = at("qkv2", [P, 26, SEQ], F32, A), at("qkv2_hi", [P, 26, SEQ], F32R, A)
    k.probs = at("probs", [P, 2, TOK], F32, H)
    k.pt6 = at("pt6", [P, 2, 2, 6, 256], F32, H + 6144)
    k.pt4 = at("pt4", [P, 2, 2, 4, 256], F32, H + 6144)
    k.qs = at("qs", [P, 2, SEQ], F32R, H + 30720)
    k.keys = at("keys", [P, 2, 2, TOK], F32R, H + 34816)
    k.keys2 = at("keys2", [P, 2, 2, SEQ], F32R, H + 34816)
    k.spread = at("spread", [P, 256], F32, H + 47104)
    k.part = at("part", [P, 256], F32, H + 48128)
    k.rot_c = at("rot_c", [P, 2, SEQ], F32, H)
    k.rot_s = at("rot_s", [P, SEQ], F32, H + 4096)
    k.rot_q = at("rot_q", [P, 2, TOK], F32, H + 6144)
    k.split_t = at("split_t", [P, 2, SEQ], F32, H + 8192)
    k.hn_sq = at("hn_sq", [P, 2, TOK], F32, H)
    k.hn_std = at("hn_std", [P, 2, TOK], F32, H + 6144)
    k.hn_r = at("hn_r", [P, TOK], F32, H + 12288)
    k.lo_0 = at("lo_0", [P, 5, TOK], F32R, A + 30720)
    k.mean = at("mean", [P, 4, TOK], F32, A + 46080)
    k.pad = at("pad", [P, 3, SEQ + 32], F32, A + 58368)
    k.inv_cnt = at("inv_cnt", [P, 4, TOK], F32, A + 64896)
    k.w_pool = at("w_pool", [P, 4, P], F32, A + 77184)
    k.v_tok0 = at("v_tok0", [P, 6, P], F32, A + 79232)
    k.lo_1 = at("lo_1", [P, 8, SEQ], F32R, A + 36864)
    k.lo_k1 = at("lo_k1", [P, 2, TOK], F32R, A + 53248)
    k.o_t1 = at("o_t1", [P, 8, SEQ], F32, A + 59392)
    k.v_tok = at("v_tok", [P, 6, 256], F32, A + 75776)
    k.lo_2 = at("lo_2", [P, 8, SEQ], F32R, A + 53248)
    k.qlat = at("qlat", [P, 8, SEQ], F32, A + 69632)
    k.iq_s = at("iq_s", [P, SEQ], F32, H)
    k.rel = at("rel", [P, 2, SEQ], F32, H + 2048)
    k.iscore = at("iscore", [P, QT, SEQ], F32, A + 69632)
    k.vb_tok = at("vb_tok", [P, QT, SEQ], F32, H + 22528)
    k.vb_s = at("vb_s", [P, QT, P], F32, H + 47104)
    k.ckv_tok = at("ckv_tok", [P, QT, P], F32, H + 43008)
    k.ckv_s = at("ckv_s", [P, SEQ], F32, H + 45056)
    k.w_uk = at("w_uk", [P, 4, P], F32, H)
    k.w_uv = at("w_uv", [P, 8, HD], F32, A + 53248)
    k.lo_3 = at("lo_3", [P, 12, SEQ], F32R, A + 43008)
    k.o_t = at("o_t", [P, 8, SEQ], F32, A + 67584)
    k.vs_tok = at("vs_tok", [P, QT, 256], F32, H + 22528)
    k.vw_tok = at("vw_tok", [P, QT, 256], F32, H + 26624 + 16384)
    k.kc2 = at("kc2", [P, 4, SEQ], F32, H)
    k.w1k = at("w1k", [P, CMP_LEN // 2, P], F32, H + 8192)
    k.w1v = at("w1v", [P, CMP_LEN // 2, P], F32, H + 26624)
    c = [C]

    def small(name, shape, dt=F32):
        size = int(np.prod(shape[1:])) * (2 if dt == BF16 else 4)
        t = at(name, shape, dt, c[0])
        c[0] += -(-size // 32) * 32
        return t

    k.table = small("table", [P, 2, 2, SEQ])
    k.ident, k.ones, k.rot_a, k.rot_b, k.block2 = (small(n, [P, P]) for n in ("ident", "ones", "rot_a", "rot_b", "block2"))
    k.masks = small("masks", [P, 5, P], BF16)
    k.masks_f = at("masks_f", [P, 5, P], F32, TMP)
    k.ident_b, k.causal, k.band_l, k.band_r = (k.masks[:, n, :] for n in range(4))
    k.cmp_mask = k.masks[:, 4, :].rearrange("p (q n) -> p q n", n=32)
    k.cmp_valid = small("cmp_valid", [P, QT])
    k.eps = small("eps", [P, 1])
    k.modv = small("modv", [P, 2 * 6 * DC, 2])
    k.b_mod = small("b_mod", [P, 2 * 6 * DC])
    k.gains = small("gains", [P, 4, 2 * DC])
    k.scale_mix, k.scale_ffn, k.gate_mix, k.gate_ffn, k.shift_mix, k.shift_ffn = (
        small(n, [P, 2, 2, DC]) for n in ("scale_mix", "scale_ffn", "gate_mix", "gate_ffn", "shift_mix", "shift_ffn"))
    k.gains2 = small("gains2", [P, 5, 1, DC])
    k.c_cols, k.silu_c = small("c_cols", [P, DC, 2]), small("silu_c", [P, DC, 2])
    k.qk_gain = small("qk_gain", [P, 3])
    k.pool_scale = small("pool_scale", [P, 4])
    k.sink, k.neg_sink = small("sink", [P, 16]), small("neg_sink", [P, 16])
    k.kv_gain, k.subln = small("kv_gain", [P, 1]), small("subln", [P, 2])
    k.lam = small("lam", [P, 4, HD])
    k.lam_p = small("lam_p", [P, 2, HD])
    k.lam_s = small("lam_s", [P, 8])
    k.nm, k.rowsum, k.den, k.sink_exp, k.rg = (small(n, [P, 2, 1]) for n in ("nm", "rowsum", "den", "sink_exp", "rg"))
    k.rinv = small("rinv", [P, 16])
    k.chosen = small("chosen", [P, QT, SEQ], BF16)
    k.iw = small("iw", [P, QT, 8])
    k.top8 = small("top8", [P, QT, 8])
    k.gates = small("gates", [P, QT, 48])
    k.gate_cmp = small("gate_cmp", [P, QT, 48])
    k.pe = small("pe", [P, 2, CMP_LEN // 2])
    k.pe_term = small("pe_term", [P, 2])
    k.w2 = small("w2", [P, 2, HD])
    k.gel = small("gel", [P, 4, 32])
    k.k_cmp = small("k_cmp", [P, 2, 32])
    k.v_cmp = small("v_cmp", [32, 256])
    k.c_m, k.c_r = small("c_m", [P, 8]), small("c_r", [P, 24])
    k.c_s, k.c_e, k.c_p = (at(n, [P, 256], F32, H + 1024 * i) for i, n in enumerate(("c_s", "c_e", "c_p")))
    k.c_pt = at("c_pt", [32, 2, SEQ], F32, H + 4096)


def split_out(k, chunk, cols, scale=None, rows=slice(0, P), bank=None):
    T = cols
    s = scale if scale is not None else 1.0

    def high(act, psum):
        return act.activation(k.h_hi[rows, chunk, T[0]:T[1]], psum, ACT.Copy, scale=s)

    def low(dve, psum):
        hi = k.h_hi[rows, chunk, T[0]:T[1]].bitcast(F32)
        if scale is None:
            return dve.tensor_tensor(k.h_lo[rows, chunk, T[0]:T[1]], psum, hi, ALU.subtract)
        return dve.scalar_tensor_tensor(k.h_lo[rows, chunk, T[0]:T[1]], psum, scale, hi, ALU.mult, ALU.subtract)
    return high, low


def plan(k, d, layers):
    ds = lambda j, at=0, n=1: slice(at + j, at + j + n) if isinstance(j, int) else bass.ds(j + at, n)
    dsx = lambda j, mul, at, n: slice(j * mul + at, j * mul + at + n) if isinstance(j, int) else bass.ds(j * mul + at, n)

    Start(k, [
        (k.x[:, :, 0:SEQ], d["x"]), (k.x[:, :, SEQ:TOK], d["ctx"]), (k.c_cols[:], d["c_cols"]), (k.c_all[:], d["c_all"]), (k.b_mod[:], d["b_mod"]),
        (k.gains[:], d["gains"]), (k.gains2[:], d["gains2"]), (k.table[:, 0], d["table_axial"]),
        (k.ident[:], d["ident"]), (k.ones[:], d["ones"]), (k.rot_a[:], d["rot_a"]), (k.rot_b[:], d["rot_b"]),
        (k.block2[:], d["block2"]), (k.masks_f[:], d["masks"]), (k.cmp_valid[:], d["cmp_valid"]), (k.eps[:], d["eps"]),
        (k.qk_gain[:, 0:2], d["qk_gain"]), (k.pool_scale[:], d["pool_scale"]), (k.sink[:], d["sink"]),
        (k.kv_gain[:], d["kv_gain"]), (k.subln[:, 0:1], d["subln"]), (k.lam[:], d["lam"]), (k.pe[:], d["pe"]), (k.w2[:], d["w2"])])
    Step(k, lambda act, chain: act.activation(k.masks[:], k.masks_f[:], ACT.Copy))
    Modulation(k, d["w_mod"], d["w_mod_rows"])

    def ffn(l, groups, mode):
        for c, (c0, c1) in enumerate(FFN_CHUNKS):
            Linear(k, d[f"ffn_in{l}_{c}"], k.h_hi, k.h_lo, groups, "gated")
            if mode == "x":
                Linear(k, d[f"ffn_out{l}_{c}"], k.act_hi, k.act_lo, groups, "add", k.x)
            else:
                Linear(k, d[f"ffn_out{l}_{c}"], k.act_hi, k.act_lo, groups, "copy" if c == 0 else "add", k.y)

    def four(n):
        return [(a, 2 * n + i, i, True) for i in range(2) for a in range(2)]

    def doubled_keys(keys, hi, lo, tile, lo_tile, cols):
        return [(keys[64 * e:64 * e + 64, a, part, cols[0]:cols[1]].unsqueeze(1), src[64 * a:64 * a + 64, t, cols[0]:cols[1]])
                for a in range(2) for part, src, t in ((0, hi, tile), (1, lo, lo_tile)) for e in range(2)]

    def split_queries(hi, lo, tile, lo_tile, col0=0, width=256):
        def stage(j, n):
            c, to = slice(col0 + width * n, col0 + width * n + width), slice(256 * n, 256 * n + width)
            return [(k.qs[64 * part:64 * part + 64, a:a + 1, to], src[64 * a:64 * a + 64, ds(j, t), c])
                    for a in range(2) for part, src, t in ((0, hi, tile), (1, lo, lo_tile))]
        return stage

    def split_scores(pe, s, q, keys, regions, masks=()):
        for c, t, width in regions:
            for part in range(2):
                ins = pe.matmul(s[:, c:c + width], q, keys[:, part, t:t + width], start=(part == 0), stop=(part == 1 and not masks), skip_group_check=True)
        for c, mask in masks:
            ins = pe.matmul(s[:, c:c + P], k.ident_b, mask, start=False, stop=True, skip_group_check=True)
        return ins

    def pair_pv(v, width, terms, pt, units):
        def pv(pe, o, j, n):
            for i, (slot, t, c0, c1) in enumerate(terms(n)):
                for a in range(2):
                    pe.matmul(o[64 * a:64 * a + 64, c0:c1], v(a, t), pt[:, n % 2, a, slot, c0:c1], start=(i == 0), stop=False, skip_group_check=True)
            for i in range(width // P):
                for a in range(2):
                    u = units(n, a, i)
                    ins = pe.matmul(o[64 * a:64 * a + 64, 256 + i * P:256 + (i + 1) * P], k.rinv[:, u:u + 1].to_broadcast([P, HD]), k.ident[:],
                                    start=True, stop=True, skip_group_check=True)
            return ins
        return pv

    def times_spread(dst, width=256):
        def finish(dve, chain, o, j, n):
            return dve.tensor_tensor(dst(j, n), o[:, 0:width].unsqueeze(1), k.spread[:, 0:width].unsqueeze(1), ALU.mult)
        return finish

    unit4 = lambda n, a, i: 4 * n + 2 * i + a
    causal_tiles = lambda qi: list(range(qi + 1))
    causal_terms = lambda n: [(t, t, P if t == 2 * n + 1 else 0, 256) for t in range(2 * n + 2)]
    in_h = lambda c, n: (k.h_hi[:, c, 0:n], k.h_lo[:, c, 0:n])
    no_marks = (lambda u: 0, 0)

    def v_batches(src, dst, tiles, col):
        made = []
        for q0 in range(0, len(tiles), 4):
            ts = tiles[q0:q0 + 4]
            made.append(([(src(t), i * P) for i, t in enumerate(ts)], P,
                         lambda dve, ps, ts=ts: dve.tensor_copy(dst[:, ts[0]:ts[-1] + 1, col:col + P], ps[:, 0:len(ts) * P].rearrange("p (t c) -> p t c", c=P)), None))
        return made

    if layers < 1:
        return
    Norm(k, "split", k.x, X_CTX, k.scale_mix[:, 0], k.shift_mix[:, 0])
    Linear(k, d["we_in"], k.h_hi, k.h_lo, X_CTX, "copy", k.qkv)
    Scale(k, lambda dve, chain: chain.link(dve.tensor_scalar(k.qk_gain[:, 2:3], k.qk_gain[:, 1:2], HD ** -0.5, None, ALU.mult)))
    HeadNorm(k, [(k.qkv[:, m, :], k.qk_gain[:, 0:1] if m < 4 else k.qk_gain[:, 2:3]) for m in range(5)], HD, k.block2[:], TOK)
    Rope(k, k.qkv, 0, 5, k.rot_a[:], k.table[:, 0], k.qkv_hi, k.lo_0, 0, TOK)
    Transposes(k, v_batches(lambda t: k.qkv[:, 5, t * P:(t + 1) * P], k.v_tok0, list(range(6)), 0))
    Load(k, [(k.inv_cnt[:], d["inv_cnt"]), (k.w_pool[:], d["w_pool"])])
    WindowMeans(k, 6)
    o0 = k.qkv[:, 6:10, :]
    Attend(k, 4, [four(0), four(1)], doubled_keys(k.keys, k.qkv_hi, k.lo_0, slice(4, 5), slice(4, 5), (0, TOK)),
           split_queries(k.qkv_hi, k.lo_0, 0, 0),
           lambda pe, s, j, a, qi: split_scores(pe, s, k.qs[:, a, qi * P:(qi + 1) * P], k.keys[:, a], [(0, 0, SEQ), (SEQ, SEQ, CTX)]),
           lambda qi: list(range(6)), lambda n, qi: 0,
           pair_pv(lambda a, t: k.v_tok0[:, t, a * HD:(a + 1) * HD], 256, lambda n: [(t, t, 0, 256) for t in range(6)], k.pt6, unit4),
           None, no_marks, times_spread(lambda j, n: o0[:, ds(j), 256 * n:256 * n + 256]), k.pt6, spread=True)
    Attend(k, 4, [[(a, 4 + n, 0, True) for a in range(2)] for n in range(2)], [], split_queries(k.qkv_hi, k.lo_0, 0, 0, SEQ, P),
           lambda pe, s, j, a, qi: split_scores(pe, s, k.qs[:, a, (qi - 4) * 256:(qi - 4) * 256 + P], k.keys[:, a], [(0, SEQ, CTX)]),
           lambda qi: [4, 5], lambda n, qi: 0,
           pair_pv(lambda a, t: k.v_tok0[:, t, a * HD:(a + 1) * HD], P, lambda n: [(0, 4, 0, P), (1, 5, 0, P)], k.pt6, lambda n, a, i: 2 * n + a),
           None, no_marks, times_spread(lambda j, n: o0[:, ds(j), SEQ + P * n:SEQ + P * n + P], P), k.pt6, spread=True)

    def pool_job(g):
        def mms(pe, ps):
            for i, (t0, t1) in enumerate(X_CTX):
                yield pe.matmul(ps[:, i, 0:t1 - t0], k.w_pool[:, g, :], k.mean[:, g, t0:t1], start=True, stop=True)
        high, low = split_out(k, 4 + g, (0, TOK), k.pool_scale[:, g:g + 1])
        return (mms, lambda dve, chain, ps: low(dve, flat(ps)[:, 0:TOK]), lambda act, ps: high(act, flat(ps)[:, 0:TOK]))

    Products(k, [pool_job(g) for g in range(4)])
    Split(k, [(o0[:, m, :], *in_h(m, TOK)) for m in range(4)])
    Linear(k, d["we_out"], k.h_hi, k.h_lo, X_CTX, "copy", k.y)
    Norm(k, "gate", k.y, X_CTX, k.gate_mix[:, 0])
    Norm(k, "split", k.x, X_CTX, k.scale_ffn[:, 0], k.shift_ffn[:, 0])
    ffn(0, X_CTX, "y")
    Norm(k, "gate", k.y, X_CTX, k.gate_ffn[:, 0])
    if layers < 2:
        return

    Norm(k, "split", k.x, X_CTX, k.scale_mix[:, 1], k.shift_mix[:, 1])
    Linear(k, d["wo_in"], k.h_hi, k.h_lo, X_CTX, "copy", k.qkv, [(0, 8, 1.0), (8, 10, HD ** -0.5), (10, 12, 1.0)])
    Rope(k, k.qkv, 0, 8, k.rot_a[:], k.table[:, 0], k.qkv_hi, k.lo_1)
    Rope(k, k.qkv, 8, 10, k.rot_a[:], k.table[:, 0], k.qkv_hi, k.lo_k1, 0, TOK)
    Transposes(k, sum((v_batches(lambda t, m=m: k.qkv[:, 10 + m, t * P:(t + 1) * P], k.v_tok, list(range(6)), m * P) for m in range(2)), []))
    Scale(k, lambda dve, chain: dve.tensor_scalar(k.neg_sink[:], k.sink[:], -1.0, None, ALU.mult))
    near = lambda qi: list(range(max(0, qi - 1), min(QT - 1, qi + 1) + 1))
    window_tiles = lambda qi: [4, 5] + near(qi) if qi < 2 else near(qi) + [4, 5]
    window_terms = lambda n: ([(0, 4, 0, 256), (1, 5, 0, 256), (2, 0, 0, 256), (3, 1, 0, 256), (4, 2, P, 256)] if n == 0 else
                              [(1, 2, 0, 256), (2, 3, 0, 256), (3, 4, 0, 256), (4, 5, 0, 256), (0, 1, 0, P)])

    def scores_window(pe, s, j, a, qi):
        tiles, regions, masks = window_tiles(qi), [], []
        for i, t in enumerate(tiles):
            if regions and i != 4 and tiles[i - 1] + 1 == t:
                regions[-1][2] += P
            else:
                regions.append([i * P, t * P, P])
            if t < 4 and t == qi - 1:
                masks.append((i * P, k.band_l))
            if t < 4 and t == qi + 1:
                masks.append((i * P, k.band_r))
        return split_scores(pe, s, k.qs[:, a, qi * P:(qi + 1) * P], k.keys[:, a], regions, masks)

    for grp in range(2):
        def sinks(j, a, grp=grp):
            at = dsx(j, 1, 8 * grp + 4 * a, 1)
            return k.neg_sink[:, at], k.sink[:, at]

        Attend(k, 4, [four(0), four(1)], doubled_keys(k.keys, k.qkv_hi, k.lo_k1, slice(8 + grp, 9 + grp), slice(grp, grp + 1), (0, TOK)),
               split_queries(k.qkv_hi, k.lo_1, 4 * grp, 4 * grp), scores_window, window_tiles, lambda n, qi: int(qi == 3),
               pair_pv(lambda a, t, grp=grp: k.v_tok[:, t, (2 * grp + a) * HD:(2 * grp + a + 1) * HD], 256, window_terms, k.pt6, unit4),
               None, no_marks, times_spread(lambda j, n, grp=grp: k.o_t1[:, ds(j, 4 * grp), 256 * n:256 * n + 256]), k.pt6, spread=True, sink=sinks)
    Split(k, [(k.o_t1[:, m, :], *in_h(m, SEQ)) for m in range(8)])
    Linear(k, d["wo_out"], k.h_hi, k.h_lo, X_ONLY, "copy", k.y)
    Norm(k, "gate", k.y, X_ONLY, k.gate_mix[:, 1])
    Norm(k, "split", k.x, X_ONLY, k.scale_ffn[:, 1], k.shift_ffn[:, 1])
    ffn(1, X_ONLY, "y")
    Norm(k, "gate", k.y, X_ONLY, k.gate_ffn[:, 1])
    if layers < 3:
        return

    Norm(k, "split", k.x, X_ONLY, k.gains2[:, 0])
    Load(k, [(k.table[:, 0], d["table64"]), (k.table[:, 1], d["table32"])])
    Linear(k, d["ev_in"], k.h_hi, k.h_lo, X_ONLY, "copy", k.qkv2,
           [(0, 1, 1.0), (1, 2, A_SCALE), (2, 3, HD ** -0.5), (3, 4, 8 ** -0.5), (4, 18, 1.0), (18, 22, HD ** -0.5), (22, 26, 1.0)])
    Rope(k, k.qkv2, 1, 2, k.rot_a[:], k.table[:, 1])
    Rope(k, k.qkv2, 12, 14, k.rot_a[:], k.table[:, 1])
    Rope(k, k.qkv2, 2, 3, k.rot_b[:], k.table[:, 0])
    Rope(k, k.qkv2, 4, 8, k.rot_b[:], k.table[:, 0])
    Rope(k, k.qkv2, 14, 22, k.rot_b[:], k.table[:, 0], k.qkv2_hi, k.lo_2)
    HeadNorm(k, [(k.qkv2[:, 0, :], k.kv_gain[:, 0:1])], P, k.ones[:], SEQ)
    Scale(k, lambda dve, chain: dve.tensor_scalar(k.ckv_s[:], k.qkv2[:, 0, :], A_SCALE, None, ALU.mult))
    Transposes(k, [([(k.qkv2[0:8, 3, t * P:(t + 1) * P], t * 8) for t in range(QT)], P,
                    lambda dve, ps: dve.tensor_copy(k.iw[:], ps[:, 0:32].rearrange("p (t h) -> p t h", h=8)), None)]
               + v_batches(lambda t: k.qkv2[:, 0, t * P:(t + 1) * P], k.ckv_tok, list(range(QT)), 0)
               + sum((v_batches(lambda t, m=m: k.qkv2[:, 22 + m, t * P:(t + 1) * P], k.vb_tok, list(range(QT)), m * P) for m in range(4)), []))
    Indexer(k, 4, k.qkv2[:, 2, :])
    TopK(k)
    Load(k, [(k.w_uk[:], d["w_uk"])])

    def lat_job(h):
        rows = slice(64 * (h % 2), 64 * (h % 2) + 64)

        def mms(pe, ps):
            yield pe.matmul(ps[:, 0, :], k.w_uk[rows, h // 2, :], k.qkv2[rows, 8 + h // 2, :], start=True, stop=True)
        return mms, lambda dve, chain, ps: dve.tensor_copy(k.qlat[:, h, :], ps[:, 0, :]), None

    Products(k, [lat_job(h) for h in range(8)])

    def scores_latent(pe, s, j, a, qi):
        rows, n, q = slice(32 * a, 32 * a + 32), (qi + 1) * P, slice(qi * P, (qi + 1) * P)
        pe.matmul(s[:, 0:n], k.qlat[:, 4 * j + a, q], k.ckv_s[:, 0:n], start=True, stop=False, skip_group_check=True)
        pe.matmul(s[:, 0:n], k.qkv2[rows, 12 + j, q], k.qkv2[rows, 1, 0:n], start=False, stop=False, skip_group_check=True, tile_position=(32 * a, 0))
        return pe.matmul(s[:, 0:n], k.ident_b, k.chosen[:, qi, 0:n], start=False, stop=True, skip_group_check=True)

    def whole_pv(v, head):
        def pv(pe, o, j, n):
            for i, (slot, t, c0, c1) in enumerate(causal_terms(n % 2)):
                ins = pe.matmul(o[:, c0:c1], v(t), k.pt4[:, n % 2, head(n), slot, c0:c1], start=(i == 0), stop=True, skip_group_check=True)
            return ins
        return pv

    Attend(k, 2, [[(n // 2, 2 * (n % 2) + i, i, True) for i in range(2)] for n in range(8)], [], lambda j, n: [], scores_latent,
           causal_tiles, lambda n, qi: 0, whole_pv(lambda t: k.ckv_tok[:, t, :], lambda n: n // 2 % 2),
           lambda dve, chain, j, u, a, qi, probs, rinv: dve.tensor_scalar(probs, probs, rinv, None, ALU.mult), no_marks,
           lambda dve, chain, o, j, n: dve.tensor_copy(k.qkv2[:, 4 + 4 * j + n // 2, 256 * (n % 2):256 * (n % 2) + 256], o[:, 0:256]), k.pt4)

    def lam_dots(dve, chain):
        chain.link(dve.tensor_tensor(k.lam_p[:], k.lam[:, 0:4:2, :], k.lam[:, 1:4:2, :], ALU.mult))
        dve.tensor_reduce(k.lam_s[:, 0:2], k.lam_p[:], AX.X, ALU.add)

    def neg_lam(dve, chain):
        chain.link(dve.tensor_tensor(k.lam_s[:, 4:5], k.lam_s[:, 3:4], k.lam_s[:, 2:3], ALU.subtract))
        chain.link(dve.tensor_scalar(k.lam_s[:, 5:6], k.lam_s[:, 4:5], -LAM_INIT, None, ALU.add))
        dve.tensor_scalar(k.subln[:, 1:2], k.subln[:, 0:1], 1.0 - LAM_INIT, None, ALU.mult)

    Scale(k, lam_dots)
    Step(k, lambda act, chain: act.activation(k.lam_s[:, 2:4], k.lam_s[:, 0:2], ACT.Exp))
    Scale(k, neg_lam)

    def causal_scores(pe, s, j, a, qi):
        n = (qi + 1) * P
        return split_scores(pe, s, k.qs[:, a, qi * P:(qi + 1) * P], k.keys2[:, a], [(0, 0, n)], [(n - P, k.causal)])

    def stage_diff(j, n):
        return (split_queries(k.qkv2_hi, k.lo_2, 14, 0)(j, n)
                + doubled_keys(k.keys2, k.qkv2_hi, k.lo_2, ds(j, 18), ds(j, 4), (256 * n, 256 * n + 256)))

    def prepare_diff(dve, chain, j, u, a, qi, probs, rinv):
        if a == 0:
            return dve.tensor_scalar(probs, probs, rinv, None, ALU.mult)
        chain.link(dve.tensor_tensor(k.rg[:, u % 2, :], rinv, k.lam_s[:, 5:6], ALU.mult))
        return dve.scalar_tensor_tensor(probs, probs, k.rg[:, u % 2, 0:1], k.probs[:, (u - 1) % 2, 0:(qi + 1) * P], ALU.mult, ALU.add)

    Attend(k, 4, [[(a, 2 * n + i, i, a == 1) for i in range(2) for a in range(2)] for n in range(2)], [], stage_diff, causal_scores,
           causal_tiles, lambda n, qi: 0, whole_pv(lambda t: k.vb_s[:, t, :], lambda n: 1), prepare_diff, (lambda u: u % 2, 0),
           lambda dve, chain, o, j, n: dve.tensor_copy(k.qkv2[:, ds(j, 14), 256 * n:256 * n + 256], o[:, 0:256].unsqueeze(1)), k.pt4,
           v_stage=lambda j: (k.vb_s[:], k.vb_tok[:, :, dsx(j, P, 0, P)]))
    HeadNorm(k, [(k.qkv2[:, 14 + m, :], k.subln[:, 1:2]) for m in range(4)], P, k.ones[:], SEQ)
    Load(k, [(k.w_uv[:], d["w_uv"])])
    Products(k, [uv_job(k, c) for c in range(4)])
    Split(k, [(k.qkv2[:, 14 + m, :], *in_h(4 + m, SEQ)) for m in range(4)])
    Linear(k, d["ev_out"], k.h_hi, k.h_lo, X_ONLY, "add", k.x)
    Norm(k, "split", k.x, X_ONLY, k.gains2[:, 2])
    ffn(2, X_ONLY, "x")
    if layers < 4:
        return

    Norm(k, "split", k.x, X_ONLY, k.gains2[:, 1])
    Linear(k, d["od_in"], k.h_hi, k.h_lo, X_ONLY, "copy", k.qkv2,
           [(0, 12, 1.0), (12, 14, HD ** -0.5), (14, 16, 1.0), (16, 18, HD ** -0.5), (18, 21, 1.0)])
    Step(k, lambda act, chain: act.activation(k.qkv2[0:48, 20, :], k.qkv2[0:48, 20, :], ACT.Sigmoid))
    Rope(k, k.qkv2, 8, 10, k.rot_b[:], k.table[:, 0])
    Load(k, [(k.w1k[:], d["w1k"]), (k.w1v[:], d["w1v"])])
    Transposes(k, [([(k.qkv2[0:48, 20, t * P:(t + 1) * P], t * 48) for t in range(QT)], P,
                    lambda dve, ps: dve.tensor_copy(k.gates[:], ps[:, 0:192].rearrange("p (t h) -> p t h", h=48)), None)]
               + sum((v_batches(lambda t, m=m: k.qkv2[:, 14 + m, t * P:(t + 1) * P], k.vs_tok, list(range(QT)), m * P) for m in range(2)), [])
               + sum((v_batches(lambda t, m=m: k.qkv2[:, 18 + m, t * P:(t + 1) * P], k.vw_tok, list(range(QT)), m * P) for m in range(2)), []))
    Scale(k, lambda dve, chain: dve.tensor_tensor(k.gate_cmp[:], k.gates[:], k.cmp_valid[:].unsqueeze(2).to_broadcast([P, QT, 48]), ALU.mult))
    for kind, (w1, src) in enumerate(((k.w1k, 8), (k.w1v, 10))):
        Doubled(k, src)
        Products(k, [compress_job(k, kind, w1)])
        Step(k, lambda act, chain, kind=kind: act.activation(
            k.gel[:, :, 0:CMP_N], k.ps[:, 0, 0:P].rearrange("p (g n) -> p g n", n=32)[:, :, 0:CMP_N], ACT.Gelu_apprx_tanh,
            bias=k.pe_term[:, kind:kind + 1]))
        Products(k, [compress_k_job(k) if kind == 0 else compress_v_job(k)])
    Rope(k, k.qkv2, 0, 8, k.rot_b[:], k.table[:, 0])
    Rope(k, k.qkv2, 12, 14, k.rot_b[:], k.table[:, 0], k.qkv2_hi, k.lo_3, 8)
    Rope(k, k.qkv2, 16, 18, k.rot_b[:], k.table[:, 0], k.qkv2_hi, k.lo_3, 10)
    CmpAttend(k, 0)
    Split(k, [(k.qkv2[:, m, :], k.qkv2_hi[:, m, :], k.lo_3[:, m, :]) for m in range(8)], in_place=True)
    for kt, v_tok, gate in ((12, k.vs_tok, 1), (16, k.vw_tok, 2)):
        for grp in range(2):
            def gated(dve, chain, j, u, a, qi, probs, rinv, grp=grp, gate=gate):
                return dve.tensor_tensor(rinv, rinv, k.gates[:, qi, dsx(j, 3, (8 * grp + 4 * a) * 3 + gate, 1)], ALU.mult)

            def add_spread(dve, chain, o, j, n, grp=grp):
                dst = k.o_t[:, ds(j, 4 * grp), 256 * n:256 * n + 256]
                chain.link(dve.tensor_tensor(k.part[:], o[:, 0:256], k.spread[:], ALU.mult))
                return dve.tensor_tensor(dst, dst, k.part[:].unsqueeze(1), ALU.add)

            lo_tile = kt // 4 * 2 + 2 + grp
            Attend(k, 4, [four(0), four(1)], doubled_keys(k.keys2, k.qkv2_hi, k.lo_3, slice(kt + grp, kt + grp + 1), slice(lo_tile, lo_tile + 1), (0, SEQ)),
                   split_queries(k.qkv2_hi, k.lo_3, 4 * grp, 4 * grp), causal_scores, causal_tiles, lambda n, qi: 0,
                   pair_pv(lambda a, t, grp=grp, v_tok=v_tok: v_tok[:, t, (2 * grp + a) * HD:(2 * grp + a + 1) * HD], 256, causal_terms, k.pt4, unit4),
                   gated, (lambda u: 0, 1), add_spread, k.pt4, spread=True)
    Split(k, [(k.o_t[:, m, :], *in_h(m, SEQ)) for m in range(8)])
    Linear(k, d["od_out"], k.h_hi, k.h_lo, X_ONLY, "add", k.x)
    Norm(k, "split", k.x, X_ONLY, k.gains2[:, 3])
    ffn(3, X_ONLY, "x")


def uv_job(k, c):
    def mms(pe, ps):
        for h in (2 * c, 2 * c + 1):
            rows = slice(64 * (h % 2), 64 * (h % 2) + 64)
            yield pe.matmul(ps[rows, 0, :], k.w_uv[:, h, :], k.qkv2[:, 4 + h, :], start=True, stop=True)
    high, low = split_out(k, c, (0, SEQ))
    return mms, lambda dve, chain, ps: low(dve, ps[:, 0, :]), lambda act, ps: high(act, ps[:, 0, :])


def compress_job(k, kind, w1):
    def mms(pe, ps):
        for l in range(CMP_LEN // 2):
            out = ps[:, 0, 0:P].rearrange("p (g n) -> p g n", n=32)[:, :, 0:CMP_N]
            yield pe.matmul(out, w1[:, l, :], k.kc2[:, :, 2 * l:2 * l + CMP_STRIDE * (CMP_N - 1) + 1:CMP_STRIDE], start=(l == 0), stop=(l == CMP_LEN // 2 - 1))
        for l in range(CMP_LEN // 2):
            yield pe.matmul(ps[:, 1, 0:1], w1[:, l, :], k.pe[:, kind, l:l + 1], start=(l == 0), stop=(l == CMP_LEN // 2 - 1))

    def out(dve, chain, ps):
        chain.link(dve.memset(k.gel[:, :, CMP_N:32], 0.0))
        return dve.tensor_copy(k.pe_term[:, kind:kind + 1], ps[:, 1, 0:1])
    return mms, out, None


def compress_k_job(k):
    def mms(pe, ps):
        for g in range(4):
            rows = slice(64 * (g % 2), 64 * (g % 2) + 64)
            yield pe.matmul(ps[rows, 0, (g // 2) * 32:(g // 2) * 32 + 32], k.w2[:, 0, :], k.gel[:, g, :], start=True, stop=True)
    return mms, lambda dve, chain, ps: dve.tensor_scalar(k.k_cmp[:], ps[:, 0, 0:64].rearrange("p (g n) -> p g n", n=32), HD ** -0.5, None, ALU.mult), None


def compress_v_job(k):
    def mms(pe, ps):
        for g in range(4):
            yield pe.matmul(ps[0:32, 0, g * HD:(g + 1) * HD], k.gel[:, g, :], k.w2[:, 1, :], start=True, stop=True)
    return mms, lambda dve, chain, ps: dve.tensor_copy(k.v_cmp[:], ps[0:32, 0, 0:256]), None


def build(nc, d, layers=5):
    with ExitStack() as ctx:
        k = Kit(nc, ctx)
        memory(k)
        k.ps = ctx.enter_context(nc.psum_tensor("ps", [P, 8, 512], F32))
        plan(k, d, layers)
        if layers > 4:
            Norm(k, "final", k.x, X_ONLY, k.gains2[:, 4], dst=k.final)
            Store(k, d["out"], k.final[:])
        else:
            Store(k, d["out"], k.x[:, :, 0:SEQ])
        names = ("pe", "act", "dve", "pool")
        done = {n: k.sem("met_" + n) for n in names}
        own = {n: k.sem("chain_" + n) for n in names}
        block = ctx.enter_context(nc.Block(no_gpsimd_drain=True))

        def meet(eng, name, n):
            eng.drain().then_inc(done[name], 1)
            for other in names:
                if other != name:
                    eng.wait_ge(done[other], n + 1)

        @block.sync
        def _(sp):
            for stage in k.stages:
                stage.sync(sp)

        @block.tensor
        def _(pe):
            for n, stage in enumerate(k.stages):
                stage.tensor(pe)
                meet(pe, "pe", n)

        @block.scalar
        def _(act):
            chain = Chain(act, own["act"])
            for n, stage in enumerate(k.stages):
                stage.scalar(act, chain)
                meet(act, "act", n)

        @block.vector
        def _(dve):
            chain = Chain(dve, own["dve"])
            for n, stage in enumerate(k.stages):
                stage.vector(dve, chain)
                meet(dve, "dve", n)

        @block.gpsimd
        def _(pool):
            chain = Chain(pool, own["pool"])
            for n, stage in enumerate(k.stages):
                stage.gpsimd(pool, chain)
                meet(pool, "pool", n)



def slabs(w, cols=None, rows=None):
    if cols is not None:
        w = w[:, cols]
    if rows is not None:
        w = w[rows[0] * P:rows[1] * P]
    kk, n = w.shape
    return np.ascontiguousarray(w.reshape(kk // P, P, n // P, P).transpose(2, 1, 0, 3)).reshape(n // P, P, kk)


def columns(v):
    v = v.reshape(v.shape[:-1] + (v.shape[-1] // P, P))
    return np.ascontiguousarray(np.moveaxis(v, -1, 0))


def heads(hs):
    return np.concatenate([np.arange(h * HD, (h + 1) * HD) for h in hs])


def tables():
    f = np.float32
    t = np.arange(SEQ)

    def table(pos_of, freqs, group):
        half = group // 2
        out = np.zeros((P, 2, SEQ), f)
        for p in range(P):
            ang = pos_of(p).astype(f) * freqs[p % group % half]
            out[p, 0], out[p, 1] = np.cos(ang), np.sin(ang)
        return out

    quarter = (f(10000.0) ** (-np.arange(16, dtype=f) / f(16))).astype(f)
    inv64 = (f(10000.0) ** (-np.arange(0, 64, 2, dtype=f) / f(64))).astype(f)
    inv32 = (f(10000.0) ** (-np.arange(0, 32, 2, dtype=f) / f(32))).astype(f)

    def rot(group):
        m = np.zeros((P, P), f)
        half = group // 2
        for p in range(P):
            if p % group < half:
                m[p + half, p] = -1
            else:
                m[p - half, p] = 1
        return m

    i, j = np.arange(P)[:, None], np.arange(P)[None, :]
    mask = lambda m: np.where(m, f(0), f(NEG)).reshape(P, P)
    tt = np.arange(SEQ).reshape(QT, P).T
    n = np.arange(32)
    cmp_ok = (n[None, None, :] * CMP_STRIDE + CMP_LEN - 1 <= tt[:, :, None]) & (n < CMP_N)
    inv = np.zeros((4, TOK), f)
    for g, w in enumerate(WINDOWS):
        for t0, t1 in ((0, SEQ), (SEQ, TOK)):
            s = np.arange(t1 - t0)
            inv[g, t0:t1] = f(1) / (np.clip(s + w - w // 2, 0, t1 - t0) - np.clip(s - w // 2, 0, t1 - t0)).astype(f)
    return {
        "table_axial": table(lambda p: t // 64 if p % 64 < 32 else t % 64, quarter, 32),
        "table64": table(lambda p: t, inv64, 64), "table32": table(lambda p: t, inv32, 32),
        "ident": np.eye(P, dtype=f), "ones": np.ones((P, P), f), "rot_a": rot(32), "rot_b": rot(64),
        "block2": ((i // HD) == (j // HD)).astype(f), 
        "masks": np.ascontiguousarray(np.stack([np.eye(P, dtype=f), mask(j <= i), mask(j >= i), mask(j <= i), mask(cmp_ok)], 1)),
        "cmp_valid": (tt >= CMP_LEN - 1).astype(f), "eps": np.full((P, 1), EPS, f),
        "inv_cnt": np.ascontiguousarray(np.broadcast_to(inv, (P, 4, TOK))),
    }


def layout(i):
    i = {n: np.asarray(a) for n, a in i.items()}
    o = tables()
    feat = lambda a: np.ascontiguousarray(a.T.reshape(DC, P, -1).transpose(1, 0, 2))
    o["x"], o["ctx"] = feat(i["x"][0]), feat(i["ctx"][0])
    o["c_cols"] = np.ascontiguousarray(np.stack([i["c"][0].reshape(DC, P), i["c_ctx"].reshape(DC, P)], -1).transpose(1, 0, 2))
    o["c_all"] = np.ascontiguousarray(np.broadcast_to(np.stack([i["c"][0], i["c_ctx"]]), (P, 2, D)))
    M = Modulation
    w = np.concatenate([i["w_mod"][0], i["w_mod"][1]], 1)
    n_x = 4 * DC
    turns = n_x // (2 * M.TURN_X)
    c0, c1 = 2 * M.TURN_PE * turns * P, 12 * D - n_x * P
    twos = lambda a: a.reshape(turns, -1, 2, P, D).transpose(0, 1, 3, 2, 4).reshape(turns, -1, P, 2 * D)
    o["w_mod"] = np.ascontiguousarray(twos(slabs(w[:, :c0]))).reshape(-1, P, 2 * D)
    o["w_mod_rows"] = np.ascontiguousarray(np.concatenate([twos(w[:, c0:c1].T), twos(w[:, c1:].T)], 1)).reshape(-1, P, 2 * D)
    o["b_mod"] = columns(i["b_mod"].reshape(-1))
    o["gains"] = np.ascontiguousarray(np.stack([columns(i[n].reshape(-1)) for n in ("g_pre_mix", "g_post_mix", "g_pre_ffn", "g_post_ffn")], 1))
    g2 = [i["norm_mix_2"][0], i["norm_mix_2"][1], i["norm_ffn_2"][0], i["norm_ffn_2"][1], i["norm_final_2"]]
    o["gains2"] = np.ascontiguousarray(np.stack([columns(g) for g in g2], 1))[:, :, None, :]
    pairs = lambda n: np.concatenate([heads((8 * (t // 4) + t % 4, 8 * (t // 4) + 4 + t % 4)) for t in range(n)])
    o["we_in"] = slabs(i["we_in"][0], np.concatenate([pairs(4), np.arange(512, 1280)]))
    o["we_out"] = slabs(i["we_out"][0][np.concatenate([pairs(4), np.arange(512, 1024)])])
    two = lambda v: np.concatenate([v, v])
    o["qk_gain"] = np.ascontiguousarray(np.stack([two(i["we_q_gain"][0]), two(i["we_k_gain"][0])], -1))
    o["w_pool"] = np.ascontiguousarray(i["we_pool"][0].transpose(1, 0, 2))
    o["pool_scale"] = columns(i["we_pool_scale"][0])
    o["wo_in"] = slabs(i["wo_in"][0], np.concatenate([pairs(8), np.arange(1024, 1536)]))
    o["wo_out"] = slabs(i["wo_out"][0][pairs(8)])
    o["sink"] = np.ascontiguousarray(np.broadcast_to(i["wo_sink"][0], (P, 16)))
    rep = lambda a, n: np.tile(a, n)
    at = np.cumsum([0, 512, 256, 128, 32, 512, 64, 8, 512, 512, 512])
    part = lambda n, times=1: rep(np.arange(at[n], at[n + 1]), times)
    o["ev_in"] = slabs(i["ev_w_in_2"][0], np.concatenate([
        part(2), part(3, 4), part(5, 2), part(6, 16), part(4), part(0), part(1), part(7), part(8), part(9)]))
    o["kv_gain"] = np.ascontiguousarray(i["ev_kv_gain_2"][0][:, None])
    o["subln"] = np.ascontiguousarray(i["ev_subln_2"][0][:, None])
    o["w_uk"] = np.ascontiguousarray(i["ev_w_uk_2"][0].reshape(4, P, P).transpose(1, 0, 2))
    o["w_uv"] = np.ascontiguousarray(i["ev_w_uv_2"][0].transpose(1, 0, 2))
    o["lam"] = np.ascontiguousarray(np.broadcast_to(i["ev_lambda_2"][0], (P, 4, HD)))
    o["ev_out"] = slabs(i["ev_w_out_2"][0])
    o["od_in"] = slabs(i["od_w_in_2"][0], np.concatenate([pairs(8), np.arange(1024, 2560), np.resize(np.arange(2560, 2608), P)]))
    o["od_out"] = slabs(i["od_w_out_2"][0][pairs(8)])
    o["pe"] = np.ascontiguousarray(i["od_cmp_pe_2"][0].reshape(2, CMP_LEN // 2, P).transpose(2, 0, 1))
    for n, w1 in zip(("w1k", "w1v"), i["od_cmp_w1_2"][0]):
        o[n] = np.ascontiguousarray(w1.reshape(CMP_LEN // 2, P, P).transpose(1, 0, 2))
    o["w2"] = np.ascontiguousarray(i["od_cmp_w2_2"][0].transpose(1, 0, 2))
    for l in range(4):
        if l < 2:
            w = i["w_ffn_in"][l]
            g, u, down = w[:, :FFN], w[:, FFN:], i["w_ffn_out"][l]
        else:
            g, u, down = i["ffn_w_gate_2"][l - 2], i["ffn_w_up_2"][l - 2], i["ffn_w_down_2"][l - 2]
        both = np.stack([slabs(g), slabs(u)], 1).reshape(2 * FC, P, D)
        for c, (c0, c1) in enumerate(FFN_CHUNKS):
            o[f"ffn_in{l}_{c}"] = both[2 * c0:2 * c1]
            o[f"ffn_out{l}_{c}"] = slabs(down, rows=(c0, c1))
    return o


def kernel(**inputs):
    from concourse.bass_utils import run_bass_kernel_spmd as run
    import concourse.bacc as bacc

    arrays = layout(inputs)
    nc = bacc.Bacc("TRN2", target_bir_lowering=False, num_devices=1)
    d = {n: nc.dram_tensor("in_" + n, a.shape, mybir.dt.from_np(a.dtype), kind="ExternalInput").ap() for n, a in arrays.items()}
    d["out"] = nc.dram_tensor("out", (P, DC, SEQ), F32, kind="ExternalOutput").ap()
    build(nc, d)
    r = run(nc, [{"in_" + n: a for n, a in arrays.items()}], core_ids=[0])
    got = r.results[0]["out"]
    return np.ascontiguousarray(got.transpose(1, 0, 2).reshape(D, SEQ).T)[None]
```
